# Optimizing a Trainium2 kernel written in Bass

```python
import math
import jax, jax.numpy as jnp
from jax import lax
import numpy as np

D_MODEL = 2048
BATCH = 1
SEQ = 256
DEPTH = 1

SB_HEADS = 8
SB_HEAD_DIM = 128
SB_WIDTH = SB_HEADS * SB_HEAD_DIM
Q_BLOCK = 128
LRU_WIDTH = 1024
LRU_BLOCKS = 8
LRU_BLOCK_DIM = LRU_WIDTH // LRU_BLOCKS
LRU_C = 8.0
CONV_W = 4
D_FF = 4 * D_MODEL
NORM_EPS = 1e-6
IN_SPLITS = [SB_WIDTH, SB_WIDTH, SB_WIDTH, LRU_WIDTH, LRU_WIDTH, D_MODEL, D_MODEL]
D_IN = sum(IN_SPLITS)
N_MOD = 6

kernel_name = "hybrid_stickbreak_rglru_block"

def rms_norm(x, g):
    xf = x.astype(jnp.float32)
    y = xf * lax.rsqrt(jnp.mean(xf * xf, axis=-1, keepdims=True) + NORM_EPS)
    return (y * g.astype(jnp.float32)).astype(x.dtype)

def split_cols(y, sizes):
    idx = np.cumsum(sizes)[:-1].tolist()
    return jnp.split(y, idx, axis=-1)

def stick_breaking_attention(q, k, v):
    B, H, S, Dh = q.shape
    nb = S // Q_BLOCK
    scale = 1.0 / math.sqrt(Dh)
    qb = q.reshape(B, H, nb, Q_BLOCK, Dh).transpose(2, 0, 1, 3, 4)
    key_pos = jnp.arange(S)

    def one_block(args):
        qi, i = args
        z = jnp.einsum('bhqd,bhkd->bhqk', qi, k).astype(jnp.float32) * scale
        q_pos = i * Q_BLOCK + jnp.arange(Q_BLOCK)
        mask = key_pos[None, :] < q_pos[:, None]
        log_beta = jax.nn.log_sigmoid(z)
        log_one_minus = jnp.where(mask, jax.nn.log_sigmoid(-z), 0.0)
        tail = lax.cumsum(log_one_minus, axis=3, reverse=True) - log_one_minus
        w = jnp.where(mask, jnp.exp(log_beta + tail), 0.0)
        return jnp.einsum('bhqk,bhkd->bhqd', w.astype(v.dtype), v)

    out = lax.map(one_block, (qb, jnp.arange(nb)))
    return out.transpose(1, 2, 0, 3, 4).reshape(B, H, S, Dh)

def causal_depthwise_conv(u, w, b):
    S = u.shape[1]
    up = jnp.pad(u, ((0, 0), (CONV_W - 1, 0), (0, 0)))
    out = b
    for tap in range(CONV_W):
        out = out + up[:, tap:tap + S, :] * w[tap]
    return out

def rg_lru(u, w_rg, b_rg, w_ig, b_ig, lam):
    B, S, W = u.shape
    ub = u.reshape(B, S, LRU_BLOCKS, LRU_BLOCK_DIM)
    r = jax.nn.sigmoid((jnp.einsum('bsnd,nde->bsne', ub, w_rg).reshape(B, S, W) + b_rg).astype(jnp.float32))
    i = jax.nn.sigmoid((jnp.einsum('bsnd,nde->bsne', ub, w_ig).reshape(B, S, W) + b_ig).astype(jnp.float32))
    log_a = LRU_C * r * jax.nn.log_sigmoid(lam.astype(jnp.float32))
    a = jnp.exp(log_a)
    mult = jnp.sqrt(-jnp.expm1(2.0 * log_a))
    bterm = mult * (i * u.astype(jnp.float32))

    def combine(e1, e2):
        a1, b1 = e1
        a2, b2 = e2
        return a1 * a2, a2 * b1 + b2

    _, h = lax.associative_scan(combine, (a, bterm), axis=1)
    return h.astype(u.dtype)

def setup_inputs(seed: int = 0) -> dict:
    key = jax.random.key(seed)
    ks = jax.random.split(key, 24)
    f32 = jnp.float32
    nrm = lambda k, shape, fan: jax.random.normal(k, shape, f32) * (fan ** -0.5)
    u = jax.random.uniform(ks[14], (DEPTH, LRU_WIDTH), f32, 0.9, 0.999)
    return {
        "x": jax.random.normal(ks[0], (BATCH, SEQ, D_MODEL), f32),
        "c": jax.random.normal(ks[1], (BATCH, D_MODEL), f32),
        "w_ada": nrm(ks[2], (DEPTH, D_MODEL, N_MOD * D_MODEL), D_MODEL) * 0.5,
        "b_ada": 0.02 * jax.random.normal(ks[3], (DEPTH, N_MOD * D_MODEL), f32),
        "norm1_g": 1.0 + 0.02 * jax.random.normal(ks[4], (DEPTH, D_MODEL), f32),
        "w_in": nrm(ks[5], (DEPTH, D_MODEL, D_IN), D_MODEL),
        "b_in": 0.02 * jax.random.normal(ks[6], (DEPTH, D_IN), f32),
        "q_norm_g": 1.0 + 0.02 * jax.random.normal(ks[7], (DEPTH, SB_HEAD_DIM), f32),
        "k_norm_g": 1.0 + 0.02 * jax.random.normal(ks[8], (DEPTH, SB_HEAD_DIM), f32),
        "conv_w": nrm(ks[9], (DEPTH, CONV_W, LRU_WIDTH), CONV_W),
        "conv_b": 0.02 * jax.random.normal(ks[10], (DEPTH, LRU_WIDTH), f32),
        "w_rg": nrm(ks[11], (DEPTH, LRU_BLOCKS, LRU_BLOCK_DIM, LRU_BLOCK_DIM), LRU_BLOCK_DIM),
        "b_rg": 0.02 * jax.random.normal(ks[12], (DEPTH, LRU_WIDTH), f32),
        "w_ig": nrm(ks[13], (DEPTH, LRU_BLOCKS, LRU_BLOCK_DIM, LRU_BLOCK_DIM), LRU_BLOCK_DIM),
        "b_ig": 0.02 * jax.random.normal(ks[15], (DEPTH, LRU_WIDTH), f32),
        "lru_lambda": jnp.log(u) - jnp.log1p(-u),
        "w_branch_a": nrm(ks[16], (DEPTH, SB_WIDTH, D_MODEL), SB_WIDTH),
        "w_branch_b": nrm(ks[17], (DEPTH, LRU_WIDTH, D_MODEL), LRU_WIDTH),
        "w_out": nrm(ks[18], (DEPTH, D_MODEL, D_MODEL), D_MODEL),
        "norm2_g": 1.0 + 0.02 * jax.random.normal(ks[19], (DEPTH, D_MODEL), f32),
        "w_mlp_in": nrm(ks[20], (DEPTH, D_MODEL, D_FF), D_MODEL),
        "w_mlp_out": nrm(ks[21], (DEPTH, D_FF, D_MODEL), D_FF),
    }

def reference(x, c, w_ada, b_ada, norm1_g, w_in, b_in, q_norm_g, k_norm_g, conv_w, conv_b,
              w_rg, b_rg, w_ig, b_ig, lru_lambda, w_branch_a, w_branch_b, w_out, norm2_g,
              w_mlp_in, w_mlp_out):
    B, S, D = x.shape
    c_act = jax.nn.silu(c)
    for l in range(DEPTH):
        mod = c_act @ w_ada[l] + b_ada[l]
        shift1, scale1, gate1, shift2, scale2, gate2 = [m[:, None, :] for m in jnp.split(mod, N_MOD, axis=-1)]

        h = rms_norm(x, norm1_g[l]) * (1.0 + scale1) + shift1
        proj = h @ w_in[l] + b_in[l]
        q, k, v, lru_x, lru_gate, gate_a, gate_b = split_cols(proj, IN_SPLITS)

        to_heads = lambda t: t.reshape(B, S, SB_HEADS, SB_HEAD_DIM).transpose(0, 2, 1, 3)
        qh = rms_norm(to_heads(q), q_norm_g[l])
        kh = rms_norm(to_heads(k), k_norm_g[l])
        vh = to_heads(v)
        att = stick_breaking_attention(qh, kh, vh)
        att = att.transpose(0, 2, 1, 3).reshape(B, S, SB_WIDTH)
        y_a = att @ w_branch_a[l]

        u = causal_depthwise_conv(lru_x, conv_w[l], conv_b[l])
        rec = rg_lru(u, w_rg[l], b_rg[l], w_ig[l], b_ig[l], lru_lambda[l])
        y_b = (rec * jax.nn.gelu(lru_gate)) @ w_branch_b[l]

        merged = jax.nn.sigmoid(gate_a) * y_a + jax.nn.sigmoid(gate_b) * y_b
        x = x + gate1 * (merged @ w_out[l])

        h2 = rms_norm(x, norm2_g[l]) * (1.0 + scale2) + shift2
        ff = jnp.square(jax.nn.relu(h2 @ w_mlp_in[l])) @ w_mlp_out[l]
        x = x + gate2 * ff
    return x


_drawn_inputs = setup_inputs


def setup_inputs(seed=0):
    import zlib

    import numpy as np

    out = dict(_drawn_inputs(seed))
    spreads = {}
    factors = {'norm1_g': 8.0,
     'b_in': 8.0,
     'q_norm_g': 22.792,
     'k_norm_g': 8.0,
     'conv_b': 8.0,
     'w_rg': 2.98,
     'b_rg': 38.035,
     'b_ig': 8.0,
     'norm2_g': 6.374}
    for name, (base, spread) in spreads.items():
        noise = np.random.default_rng([zlib.crc32(name.encode()), seed]).standard_normal(out[name].shape)
        drawn = base * np.exp(spread * noise) if base else spread * noise
        out[name] = __import__('jax').numpy.asarray(drawn.astype(out[name].dtype))
    for name, factor in factors.items():
        out[name] = (out[name] * factor).astype(out[name].dtype)
    return out
```

```python
import math
from contextlib import ExitStack

import concourse.bass as bass
from concourse import mybir

F32 = mybir.dt.float32
F32R = mybir.dt.float32r
ACT = mybir.ActivationFunctionType
ALU = mybir.AluOpType
ds = bass.ds

P = 128
EPS = 1e-6
LRU_C = 8.0


def hybrid_block(nc, x, c, w_ada, b_ada, norm1_g, w_in, b_in, q_norm_g, k_norm_g, conv_w, conv_b,
                 w_rg, b_rg, w_ig, b_ig, lru_lambda, w_branch_a, w_branch_b, w_out, norm2_g,
                 w_mlp_in, w_mlp_out, out):
    S, D = x.shape[1], x.shape[2]
    W = conv_w.shape[2]
    HD = q_norm_g.shape[1]
    DFF = w_mlp_in.shape[2]
    TAPS = conv_w.shape[1]
    KT = D // P
    NT = W // P
    TOK = S // P
    PAN = 256
    CH = 4
    KC = KT // CH
    AB = 1024
    NMOD = w_ada.shape[2]
    assert S == 256 and HD == P and PAN == 2 * P and KT == 16 and NT == 8 and TAPS == 4

    NPW = W // PAN
    NPD = D // PAN
    P_LX, P_LG = 0, NPW
    P_Q, P_K, P_V = 2 * NPW, 3 * NPW, 4 * NPW
    P_GA = 5 * NPW
    P_GB = P_GA + NPD
    P_BR = P_GB + NPD
    P_OUT = P_BR + NPD
    P_MLP = P_OUT + NPD
    GROUPS = DFF // D
    N_PANELS = P_MLP + GROUPS * 2 * NPD
    C_Q, C_K, C_V, C_LX, C_LG, C_GA, C_GB = 0, W, 2 * W, 3 * W, 4 * W, 5 * W, 5 * W + D
    PRO_BLOCKS = 2 * D // AB
    PRO_ADA = PRO_BLOCKS * KT

    w_ada_v = w_ada[0]
    w_in_v = w_in[0].rearrange("(t p) n -> p t n", p=P)
    w_ba_v = w_branch_a[0].rearrange("(t p) n -> p t n", p=P)
    w_bb_v = w_branch_b[0].rearrange("(t p) n -> p t n", p=P)
    w_out_v = w_out[0].rearrange("(t p) n -> p t n", p=P)
    w_mi_v = w_mlp_in[0].rearrange("(t p) n -> p t n", p=P)
    w_mo_v = w_mlp_out[0].rearrange("(t p) n -> p t n", p=P)
    w_rg_v = w_rg[0].rearrange("n d e -> d n e")
    w_ig_v = w_ig[0].rearrange("n d e -> d n e")
    out_v = out[0].rearrange("(b p) n -> p b n", p=P)

    with ExitStack() as ctx:
        base = (nc.sbuf_base + 31) // 32 * 32
        top = [base]

        def at(name, shape, offset, dt=F32):
            return nc.alloc_sbuf_tensor_at(name, [P] + shape, dt, offset=offset)

        def new(name, shape, dt=F32):
            o = top[0]
            top[0] += (4 * math.prod(shape) + 31) // 32 * 32
            return at(name, shape, o, dt)

        def region(nbytes):
            o = top[0]
            top[0] += nbytes
            return o

        TILE = 4 * S
        raw = new("raw_w", [CH, KC * PAN])
        w_hi = new("w_hi", [CH, KC * PAN], F32R)
        w_lo = new("w_lo", [CH, KC * PAN], F32R)
        ada_w = new("ada_w", [2, AB])
        ada_acc = new("ada_acc", [AB])
        actv = new("actv", [KT, 2, S], F32R)
        xT = new("xT", [KT, S])
        r_mix = region(4 * NT * TILE)
        r_lg = r_mix + NT * TILE
        r_qk = r_mix + 2 * NT * TILE
        lx = at("lru_x", [NT, S], r_mix)
        lg = at("lru_gate", [NT, S], r_lg)
        yb = at("yb_in", [NT, 2, S], r_mix, F32R)
        qk = at("qk", [NT, 2, S], r_qk)
        att = at("att", [NT, 2, S], r_qk, F32R)
        hid = at("hidden", [KT, 2, S], r_mix, F32R)
        pro_w = at("pro_w", [8, AB], r_mix)
        vT = new("vT", [NT, S])
        r_gate = region(2 * KT * TILE)
        gates = at("gates", [2, KT, S], r_gate)
        x_rows = at("x_rows", [TOK, D], r_gate)
        vec_rows = at("vec_rows", [3, P], r_gate + 4 * TOK * D)
        pro_acc = at("pro_acc", [2, AB], r_gate + 4 * TOK * D + 2048)
        lru_u = at("lru_u", [NT, S], r_gate)
        lru_r = at("lru_r", [NT, S], r_gate + NT * TILE)
        lru_iu = at("lru_iu", [NT, S], r_gate + 2 * NT * TILE)
        lru_a = at("lru_a", [NT, S], r_gate + 3 * NT * TILE)
        mlp_acc = at("mlp_acc", [KT, S], r_gate)
        half = new("half", [2, S])
        t1 = new("t1", [2, S])
        t2 = new("t2", [2, S])
        t3 = new("t3", [2, S])
        lru_w = new("lru_w", [4, P])
        ident = new("ident", [P])
        ones = new("ones", [P])
        neg_tri = new("neg_tri", [P])
        neg_one = new("neg_one", [P])
        cols = new("cols", [3 * P])
        c_act = new("c_act", [KT])
        mod = new("mod", [NMOD // P])
        sg = new("sg", [2, KT])
        c8 = new("c8", [NT])
        gqk = new("gqk", [2])
        eps = new("eps", [1])
        tiny = new("tiny", [8, NT])
        qn = new("qn", [2, S])
        lsum = new("lsum", [3 * P])
        wgt = new("wgt", [3 * P])
        v_col = new("v_col", [S])
        v_row = new("v_row", [TOK, P])
        zr = new("zr", [3 * P])
        out_rows = new("out_rows", [2, TOK, PAN])
        assert top[0] <= nc.sbuf_usable_end, top[0] - nc.sbuf_usable_end
        ctx.enter_context(nc.sbuf_tensor("arena", [P, (top[0] - base) // 4 + 8], F32))

        pm = ctx.enter_context(nc.psum_tensor("panel_sums", [P, 4, 512], F32))
        ps = ctx.enter_context(nc.psum_tensor("side_sums", [P, 4, 512], F32))

        C_C, C_BADA, C_N1 = 0, KT, KT + NMOD // P
        C_BIN, C_N2, C_CW, C_CB = P, P + 72, P + 88, P + 120
        C_BRG, C_BIG, C_LAM, C_GQ = 2 * P, 2 * P + NT, 2 * P + 2 * NT, 2 * P + 3 * NT
        assert C_N1 + KT == P and NMOD // P == 96 and w_in.shape[2] // P == 72

        def sem(name):
            return ctx.enter_context(nc.semaphore(name))

        started = []

        def sem1(name):
            started.append(sem(name))
            return started[-1]

        raw_in = [sem(f"raw_in{s}") for s in range(CH)]
        ada_in = [sem(f"ada_in{s}") for s in range(2)]
        pro_in = [sem(f"pro_in{s}") for s in range(8)]
        x_in = [sem(f"x_in{b}") for b in range(TOK)]
        vec_zero = sem("vec_zero")
        vec_in = sem("vec_in")
        consts = sem("consts")
        hi_done = sem("hi_done")
        lo_done = sem("lo_done")
        mm_done = sem("mm_done")
        half_done = sem("half_done")
        evac_done = sem("evac_done")
        bhalf_done = sem("bhalf_done")
        bevac_done = sem1("bevac_done")
        ada_done = sem("ada_done")
        ada_sum = sem("ada_sum")
        mod_done = sem1("mod_done")
        act_ready = sem1("act_ready")
        vec_t = sem("vec_t")
        vec_c = sem("vec_c")
        x_t = sem("x_t")
        x_c = sem("x_c")
        x_sq = sem("x_sq")
        ssq = sem("ssq")
        rstd = sem("rstd")
        nrm_t = sem("nrm_t")
        nrm_h = sem("nrm_h")
        silu = sem("silu")
        small = sem("small")
        conv_0 = sem("conv_0")
        conv_s = sem("conv_s")
        gelu_done = sem("gelu_done")
        lru_w_in = sem("lru_w_in")
        ri_mm = sem1("ri_mm")
        ri_sig = sem1("ri_sig")
        iu_done = sem("iu_done")
        lru_t = sem("lru_t")
        lru_m = sem1("lru_m")
        lru_q = sem("lru_q")
        lru_s = sem("lru_s")
        yb_hi = sem("yb_hi")
        yb_ready = sem("yb_ready")
        hd_sq = sem("hd_sq")
        hd_ssq = sem1("hd_ssq")
        hd_ln = sem("hd_ln")
        hd_rs = sem("hd_rs")
        hd_qn = sem1("hd_qn")
        hd_vc = sem("hd_vc")
        hd_vt = sem1("hd_vt")
        hd_vr = sem("hd_vr")
        hd_z = sem("hd_z")
        hd_r = sem("hd_r")
        hd_sp = sem("hd_sp")
        hd_l = sem1("hd_l")
        hd_lm = sem("hd_lm")
        hd_tail = sem1("hd_tail")
        hd_e = sem1("hd_e")
        hd_w = sem("hd_w")
        hd_att = sem1("hd_att")
        hd_ah = sem("hd_ah")
        hd_al = sem1("hd_al")
        sga = sem("sga")
        mrg = sem("mrg")
        mrg_h = sem("mrg_h")
        res = sem("res")
        sq2 = sem1("sq2")
        ssq2 = sem("ssq2")
        hid_h = sem("hid_h")
        out_t = sem("out_t")
        out_c = sem("out_c")
        act_passed, pool_passed = sem("act_passed"), sem("pool_passed")
        out_d = [sem(f"out_d{b}") for b in range(2)]

        def reach(eng, s, v):
            if isinstance(v, int) and v <= 0:
                return
            eng.wait_ge(s, v + 1 if s in started else v)

        def start(eng, sems):
            for s in sems:
                eng.sem_inc(s, 1)

        def passed(eng, s):
            eng.sem_inc(s, 1)

        def flat(t, off, n):
            v = t[:]
            if len(v.shape) == 3:
                v = v.rearrange("p a b -> p (a b)")
            elif len(v.shape) == 4:
                v = v.rearrange("p a b c -> p (a b c)")
            return v[:, ds(off, n)]

        BW, BD = NPW // 2, NPD // 2

        N_SER = 9
        SMALL_CACT = 3
        SMALL_C8 = SMALL_CACT + 4 + 1 + 2 * (N_SER - 2) + 4
        SMALL_GQK = SMALL_C8 + 2
        SMALL_ACC = SMALL_GQK + 2
        SMALL_T2 = SMALL_ACC + 5 + 1

        block = ctx.enter_context(nc.Block())

        @block.sync
        def _(sp):
            def pro_load(b, q, first):
                src = w_ada_v[q * P:(q + 1) * P, ds(sp.snap(b * AB) if not isinstance(b, int) else b * AB, AB)]
                if not first:
                    sp.wait_ge(ada_done, b * KT + q - 7)
                sp.dma_start(pro_w[:, q % 8, :], src).then_inc(pro_in[q % 8], 16)

            for b in range(TOK):
                sp.dma_start(x_rows[:, b, :], x[0, b * P:(b + 1) * P, :]).then_inc(x_in[b], 16)
            for q in range(KT):
                pro_load(0, q, q < 8)
            with sp.Fori(1, PRO_BLOCKS) as b:
                for q in range(KT):
                    pro_load(b, q, False)

            def load(p, k, view, t0, nt, col, slot_off=0):
                if not isinstance(col, int):
                    col = sp.snap(col)
                src = view[:, ds(t0, nt), ds(col, PAN)] if not isinstance(t0, int) else view[:, t0:t0 + nt, ds(col, PAN)]
                reach(sp, lo_done, CH * (p - 1) + k + 1)
                sp.dma_start(raw[:, k, :].rearrange("p (t n) -> p t n", n=PAN), src).then_inc(raw_in[k], 16)

            def stage(p0, bodies, view, c0):
                with sp.Fori(0, bodies) as i:
                    for j in range(2):
                        for k in range(CH):
                            load(p0 + 2 * i + j, k, view, KC * k, KC, c0 + PAN * (2 * i + j))

            for j in range(2):
                for k in range(CH):
                    load(j, k, w_in_v, KC * k, KC, C_LX + PAN * j)
            for j in range(2, NPW):
                for k in range(CH):
                    load(j, k, w_in_v, KC * k, KC, C_LX + PAN * j)
            stage(P_LG, BW, w_in_v, C_LG)
            with sp.Fori(0, BW) as i:
                for j in range(2):
                    n = sp.snap(2 * (2 * i + j))
                    for k in range(CH):
                        load(P_Q + 2 * i + j, k, w_in_v, KC * k, KC, C_Q + PAN * (2 * i + j))
                    src_r, src_i = w_rg_v[:, ds(n, 2), :], w_ig_v[:, ds(n, 2), :]
                    reach(sp, ri_mm, 2 * i + j)
                    sp.dma_start(lru_w[:, 0:2, :], src_r).then_inc(lru_w_in, 16)
                    sp.dma_start(lru_w[:, 2:4, :], src_i).then_inc(lru_w_in, 16)
            stage(P_K, BW, w_in_v, C_K)
            stage(P_V, BW, w_in_v, C_V)
            stage(P_GA, BD, w_in_v, C_GA)
            stage(P_GB, BD, w_in_v, C_GB)
            with sp.Fori(0, BD) as i:
                for j in range(2):
                    for k in range(CH):
                        view = w_bb_v if k < 2 else w_ba_v
                        load(P_BR + 2 * i + j, k, view, KC * (k % 2), KC, PAN * (2 * i + j))
            stage(P_OUT, BD, w_out_v, 0)
            def mlp_in(g):
                with sp.Fori(0, BD) as i:
                    for j in range(2):
                        for k in range(CH):
                            load(P_MLP + 2 * NPD * g + 2 * i + j, k, w_mi_v, KC * k, KC,
                                 D * g + PAN * (2 * i + j))

            with sp.Fori(0, GROUPS - 1) as g:
                mlp_in(g)
                with sp.Fori(0, BD) as i:
                    for j in range(2):
                        for k in range(CH):
                            load(P_MLP + 2 * NPD * g + NPD + 2 * i + j, k, w_mo_v, sp.snap(KT * g + KC * k), KC,
                                 PAN * (2 * i + j))
            mlp_in(GROUPS - 1)
            LAG = 3
            for q in range(NPD + LAG):
                if q < NPD:
                    for k in range(CH):
                        load(N_PANELS - NPD + q, k, w_mo_v, KT * (GROUPS - 1) + KC * k, KC, PAN * q)
                if q >= LAG:
                    r = q - LAG
                    sp.wait_ge(out_c, r + 1)
                    sp.dma_start(out_v[:, :, PAN * r:PAN * (r + 1)], out_rows[:, r % 2, :, :]).then_inc(out_d[r % 2], 16)
            for b in range(2):
                sp.wait_ge(out_d[b], 16 * BD)

        @block.gpsimd
        def _(pool):
            nc.gpsimd.memset(vec_rows[:, :, :], 0.0).then_inc(vec_zero, 1)
            nc.gpsimd.memset(ident[:, :], 0.0).then_inc(consts, 1)
            nc.gpsimd.memset(ones[:, :], 1.0).then_inc(consts, 1)
            nc.gpsimd.memset(neg_one[:, :], -1.0).then_inc(consts, 1)
            nc.gpsimd.memset(eps[:, :], EPS).then_inc(consts, 1)
            pool.wait_ge(consts, 4)
            nc.gpsimd.affine_select(out=ident[:, :], in_=ident[:, :], compare_op=ALU.not_equal, fill=1.0, base=0,
                                    pattern=[[-1, P]], channel_multiplier=1).then_inc(consts, 1)
            nc.gpsimd.affine_select(out=neg_tri[:, :], in_=neg_one[:, :], compare_op=ALU.is_ge, fill=0.0, base=0,
                                    pattern=[[-1, P]], channel_multiplier=1).then_inc(consts, 1)

            def diag(t):
                return t[:, :].rearrange("p (a b) -> p a b", b=P)[:, 0:3:2, :]

            with pool.Fori(0, NT) as h:
                reach(pool, hd_l, h + 1)
                passed(pool, pool_passed)
                nc.gpsimd.affine_select(out=diag(lsum), in_=diag(lsum), compare_op=ALU.is_gt, fill=0.0, base=0,
                                        pattern=[[0, 2], [1, P]], channel_multiplier=-1).then_inc(hd_lm, 1)
                reach(pool, hd_e, h + 1)
                passed(pool, pool_passed)
                nc.gpsimd.affine_select(out=diag(wgt), in_=diag(wgt), compare_op=ALU.is_gt, fill=0.0, base=0,
                                        pattern=[[0, 2], [1, P]], channel_multiplier=-1).then_inc(hd_w, 1)

        @block.scalar
        def _(act):
            A = nc.scalar.activation
            start(act, [ri_sig, hd_e, sq2])

            act.wait_ge(vec_zero, 1)
            def rows(v, g, r):
                n = 1
                for s in v.shape:
                    n *= s
                n //= P
                while len(v.shape) > 2:
                    v = v.rearrange("a b c -> (a b) c")
                act.dma_start(vec_rows[r:r + n, g, :], v.rearrange("a (t p) -> (a t) p", p=P)).then_inc(vec_in, 16)

            rows(c, 0, 0)
            rows(b_ada, 0, C_BADA)
            rows(norm1_g, 0, C_N1)
            rows(b_in, 1, 0)
            rows(norm2_g, 1, C_N2 - P)
            rows(conv_w, 1, C_CW - P)
            rows(conv_b, 1, C_CB - P)
            rows(b_rg, 2, 0)
            rows(b_ig, 2, NT)
            rows(lru_lambda, 2, 2 * NT)
            rows(q_norm_g, 2, 3 * NT)
            rows(k_norm_g, 2, 3 * NT + 1)
            act.wait_ge(vec_t, 3)
            A(cols[:, :], ps[:, 0, 0:3 * P], ACT.Copy).then_inc(vec_c, 1)
            act.wait_ge(vec_c, 1)
            A(tiny[:, 0:2, :].rearrange("p a b -> p (a b)"), cols[:, 0:KT], ACT.Exp, scale=-1.0).then_inc(silu, 1)
            A(tiny[:, 2, :], cols[:, C_LAM:C_LAM + NT], ACT.Abs).then_inc(silu, 1)
            act.wait_ge(silu, 2)
            A(tiny[:, 3, :], tiny[:, 2, :], ACT.Exp, scale=-1.0).then_inc(silu, 1)
            for b in range(KT // 2):
                act.wait_ge(x_t, b + 1)
                A(xT[:, 2 * b:2 * b + 2, :], pm[:, b % 4, :].rearrange("p (a t) -> p a t", a=2),
                  ACT.Copy).then_inc(x_c, 1)
                if b >= 2:
                    act.wait_ge(ssq, b - 1)
                act.wait_ge(x_c, b + 1)
                A((t1, t2)[b % 2][:, :, :], xT[:, 2 * b:2 * b + 2, :], ACT.Square).then_inc(x_sq, 1)
            act.wait_ge(ssq, KT // 2)
            A(t3[:, 0, :], ps[:, 1, 0:S], ACT.Sqrt, scale=1.0 / D, bias=eps[:, 0:1]).then_inc(rstd, 1)

            def hi_chunk(p, k):
                act.wait_ge(raw_in[k], 16 * (p + 1))
                reach(act, mm_done, CH * (p - 1) + k + 1)
                A(w_hi[:, k, :], raw[:, k, :], ACT.Copy).then_inc(hi_done, 1)

            def norm_hi(which, n0):
                sh = 0 if which == 0 else 3 * KT
                with act.Fori(0, KT // 2) as i:
                    for j in range(2):
                        act.wait_ge(nrm_t, n0 + 2 * i + j + 1)
                        reach(act, mod_done, PRO_BLOCKS)
                        passed(act, act_passed)
                        A(actv[:, ds(2 * i + j, 1), 0, :], (t1, t2)[j][:, 0:1, :], ACT.Identity,
                          bias=mod[:, ds(sh + 2 * i + j, 1)]).then_inc(nrm_h, 1)

            def half_copy(p, bias_col=None):
                b0 = 2 * (p[1] % 2)
                pp = p[0]
                if bias_col is None:
                    reach(act, evac_done, pp)
                    act.wait_ge(mm_done, CH * pp + CH)
                    A(half[:, :, :], pm[:, b0:b0 + 2, S:2 * S], ACT.Copy).then_inc(half_done, 1)
                else:
                    for t in range(2):
                        if t == 0:
                            reach(act, evac_done, pp)
                            act.wait_ge(mm_done, CH * pp + CH)
                            passed(act, act_passed)
                        m = A(half[:, t, :], pm[:, b0 + t, S:2 * S], ACT.Identity,
                              bias=cols[:, ds(C_BIN + bias_col + t, 1)])
                    m.then_inc(half_done, 1)

            def ada_load(p, j, m, blk, kt0):
                for a in range(2):
                    src = w_ada_v[ds(act.snap((kt0 + a) * P) if not isinstance(kt0, int) else (kt0 + a) * P, P),
                                  blk * AB:(blk + 1) * AB]
                    reach(act, ada_done, PRO_ADA + m + a - 1)
                    act.dma_start(ada_w[:, a, :], src).then_inc(ada_in[a], 16)

            def stage(p0, bodies, ada=None, pre=None, mid=None, post=None, bias=None, last=False, lo=0, evac=True):
                def body(i):
                    for j in range(2):
                        q = 2 * i + j
                        p = p0 + q
                        if ada:
                            ada_load(p, j, ada[0] + 2 * q, ada[1], ada[2] + 2 * q)
                        if pre:
                            pre(i, j, q)
                        for k in range(CH):
                            hi_chunk(p + 1, k)
                            if mid:
                                mid(i, j, q, k, p)
                        if evac:
                            half_copy((p, j), None if bias is None else bias + 2 * q)
                        if post:
                            post(i, j, q)
                if isinstance(bodies, list):
                    for i in bodies:
                        body(i)
                else:
                    with act.Fori(lo, bodies) as i:
                        body(i)

            for k in range(CH):
                hi_chunk(0, k)
            norm_hi(0, 0)
            T_LX, T_LG, T_GA, T_GB = C_LX // P, C_LG // P, C_GA // P, C_GB // P
            stage(P_LX, [0, 1], ada=(0, 4, 0), bias=T_LX)

            def conv0(i, j, q):
                for n in range(2):
                    act.wait_ge(evac_done, NPW)
                    A(lru_u[:, ds(2 * q + n, 1), :], lx[:, ds(2 * q + n, 1), :], ACT.Identity,
                      scale=cols[:, ds(C_CW + (TAPS - 1) * NT + 2 * q + n, 1)],
                      bias=cols[:, ds(C_CB + 2 * q + n, 1)]).then_inc(conv_0, 1)
            stage(P_LG, BW, ada=(8, 4, 8), pre=conv0, bias=T_LG)
            act.wait_ge(evac_done, P_Q)
            A(lg[:, :, :], lg[:, :, :], ACT.Gelu_apprx_tanh).then_inc(gelu_done, 1)

            def sigm(i, j, q, k, p):
                if k != 2:
                    return
                for g, dst, b in ((0, lru_r, C_BRG), (1, lru_iu, C_BIG)):
                    for n in range(2):
                        reach(act, ri_mm, q + 1)
                        passed(act, act_passed)
                        A(dst[:, ds(2 * q + n, 1), :], ps[:, g:g + 1, n * S:(n + 1) * S], ACT.Sigmoid,
                          bias=cols[:, ds(b + 2 * q + n, 1)]).then_inc(ri_sig, 1)
            stage(P_Q, BW, ada=(16, 5, 0), mid=sigm, bias=C_Q // P)

            def decay(i, j, q):
                reach(act, lru_m, 2 * q)
                act.wait_ge(small, SMALL_C8)
                reach(act, ri_sig, 4 * NPW)
                passed(act, act_passed)
                for n in range(2):
                    A(lru_a[:, ds(2 * q + n, 1), :], lru_r[:, ds(2 * q + n, 1), :], ACT.Exp,
                      scale=c8[:, ds(2 * q + n, 1)]).then_inc(lru_t, 1)
                act.wait_ge(lru_t, 5 * q + 2)
                passed(act, act_passed)
                for n in range(2):
                    A(lru_r[:, ds(2 * q + n, 1), :], lru_r[:, ds(2 * q + n, 1), :], ACT.Tanh,
                      scale=c8[:, ds(2 * q + n, 1)]).then_inc(lru_t, 1)
                act.wait_ge(lru_t, 5 * q + 4)
                passed(act, act_passed)
                A(t1[:, :, :], lru_r[:, ds(2 * q, 2), :], ACT.Identity, scale=-1.0, bias=1.0).then_inc(lru_t, 1)
            stage(P_K, BW, ada=(24, 5, 8), pre=decay, bias=C_K // P)

            def mult(i, j, q):
                reach(act, lru_m, 2 * NPW)
                A(lru_r[:, ds(2 * q, 2), :], lru_r[:, ds(2 * q, 2), :], ACT.Sqrt).then_inc(lru_q, 1)

            def rec_hi(i, j, q):
                act.wait_ge(lru_s, 4 * q + 4)
                passed(act, act_passed)
                A(yb[:, ds(2 * q, 2), 0, :], t1[:, :, :], ACT.Copy).then_inc(yb_hi, 1)
            stage(P_V, BW, pre=mult, post=rec_hi, bias=C_V // P)

            def head(h0):
                def pre(i, j, q):
                    h = i + h0
                    if j == 0:
                        reach(act, hd_ssq, h)
                        act.wait_ge(yb_ready, NPW)
                        act.wait_ge(evac_done, P_GA)
                        passed(act, act_passed)
                        A(t1[:, :, :], qk[:, ds(h, 1), :, :], ACT.Square).then_inc(hd_sq, 1)
                        reach(act, hd_vt, h)
                        passed(act, act_passed)
                        A(v_col[:, :], vT[:, ds(h, 1), :], ACT.Copy).then_inc(hd_vc, 1)
                    else:
                        act.wait_ge(hd_z, h + 1)
                        reach(act, hd_l, h)
                        A(zr[:, :], ps[:, 1, 0:3 * P], ACT.Relu).then_inc(hd_r, 1)
                        reach(act, hd_att, h)
                        A(wgt[:, :], ps[:, 1, 0:3 * P], ACT.Abs).then_inc(hd_r, 1)
                        act.wait_ge(hd_r, 5 * h + 2)
                        A(wgt[:, :], wgt[:, :], ACT.Exp, scale=-1.0).then_inc(hd_r, 1)
                        act.wait_ge(hd_r, 5 * h + 3)
                        A(wgt[:, :], wgt[:, :], ACT.Ln, bias=1.0).then_inc(hd_r, 1)

                def mid(i, j, q, k, p):
                    h = i + h0
                    if j == 0 and k == 1:
                        reach(act, hd_ssq, h + 1)
                        reach(act, hd_qn, 2 * h)
                        A(t2[:, :, :], ps[:, 0, :].rearrange("p (a t) -> p a t", a=2), ACT.Ln, scale=1.0 / HD,
                          bias=eps[:, 0:1]).then_inc(hd_ln, 1)
                        act.wait_ge(hd_ln, h + 1)
                        A(t2[:, :, :], t2[:, :, :], ACT.Exp, scale=-0.5).then_inc(hd_rs, 1)
                    if j == 0 and k == 2:
                        reach(act, hd_vt, h + 1)
                        reach(act, hd_att, h)
                        A(v_row[:, :, :], ps[:, 2, 0:S].rearrange("p (a d) -> p a d", a=TOK), ACT.Copy).then_inc(hd_vr, 1)
                    if j == 1 and k == 2:
                        reach(act, hd_tail, h + 1)
                        reach(act, hd_l, h + 1)
                        A(zr[:, :], ps[:, 1, 0:3 * P], ACT.Relu, scale=-1.0).then_inc(hd_r, 1)
                        act.wait_ge(hd_r, 5 * h + 5)
                        A(wgt[:, :], zr[:, :], ACT.Exp, scale=-1.0).then_inc(hd_e, 1)

                def post(i, j, q):
                    h = i + h0
                    if j == 1:
                        reach(act, hd_att, h + 1)
                        passed(act, act_passed)
                        A(att[:, ds(h, 1), 0, :], ps[:, 3:4, 0:S], ACT.Copy).then_inc(hd_ah, 1)
                return pre, mid, post

            pre, mid, post = head(0)
            stage(P_GA, BD, ada=(32, 6, 0), pre=pre, mid=mid, post=post, bias=T_GA)
            pre, mid, post = head(NT // 2)
            stage(P_GB, BD, ada=(48, 7, 0), pre=pre, mid=mid, post=post, bias=T_GB)

            def gate_sig(i, j, q):
                for g in (1, 0):
                    act.wait_ge(evac_done, P_BR)
                    A(gates[:, g, ds(2 * q, 2), :], gates[:, g, ds(2 * q, 2), :], ACT.Sigmoid).then_inc(sga, 1)

            def b_half(i, j, q, k, p):
                if k == 1:
                    act.wait_ge(evac_done, p)
                    act.wait_ge(mm_done, CH * p + 2)
                    A(half[:, :, :], pm[:, 0:2, S:2 * S], ACT.Copy).then_inc(bhalf_done, 1)
                if k == 3:
                    reach(act, bevac_done, q + 1)
                    act.wait_ge(mm_done, CH * p + 4)
                    A(half[:, :, :], pm[:, 2:4, S:2 * S], ACT.Copy).then_inc(half_done, 1)

            def merged_hi(i, j, q):
                act.wait_ge(mrg, 5 * q + 5)
                passed(act, act_passed)
                A(actv[:, ds(2 * q, 2), 0, :], t2[:, :, :], ACT.Copy).then_inc(mrg_h, 1)
            stage(P_BR, BD, ada=(64, 8, 0), pre=gate_sig, mid=b_half, post=merged_hi, evac=False)

            def square(i, j, q):
                act.wait_ge(res, 3 * q + 3)
                act.wait_ge(ssq2, q + 1)
                passed(act, act_passed)
                A(t2[:, :, :], xT[:, ds(2 * q, 2), :], ACT.Square).then_inc(sq2, 1)
            stage(P_OUT, BD, ada=(80, 9, 0), post=square)
            act.wait_ge(ssq2, NPD + 1)
            A(t3[:, 0, :], ps[:, 0, 0:S], ACT.Sqrt, scale=1.0 / D, bias=eps[:, 0:1]).then_inc(rstd, 1)
            norm_hi(1, KT)

            def hid_hi(n0):
                def f(i, j, q):
                    act.wait_ge(res, n0 + 2 * q + 2)
                    passed(act, act_passed)
                    A(hid[:, ds(2 * q, 2), 0, :], t2[:, :, :], ACT.Copy).then_inc(hid_h, 1)
                return f

            R0 = 3 * NPD
            RG = 4 * NPD
            stage(P_MLP, BD, ada=(96, 10, 0), post=hid_hi(R0))
            stage(P_MLP + NPD, BD, ada=(112, 11, 0))
            with act.Fori(1, GROUPS - 1) as g:
                stage(P_MLP + 2 * NPD * g, BD, post=hid_hi(R0 + RG * g))
                stage(P_MLP + 2 * NPD * g + NPD, BD)
            stage(P_MLP + 2 * NPD * (GROUPS - 1), BD, post=hid_hi(R0 + RG * (GROUPS - 1)))

            PF = N_PANELS - NPD

            def out_copy(q, j):
                act.wait_ge(out_t, q + 1)
                reach(act, out_d[j], 16 * (q // 2) if isinstance(q, int) else 8 * (q - j))
                A(out_rows[:, j, :, :], ps[:, 1, :].rearrange("p (b n) -> p b n", b=TOK), ACT.Copy).then_inc(out_c, 1)

            for q in range(NPD):
                if q + 1 < NPD:
                    for k in range(CH):
                        hi_chunk(PF + q + 1, k)
                        if k == 2 and q > 0:
                            out_copy(q - 1, (q - 1) % 2)
                elif q > 0:
                    out_copy(q - 1, (q - 1) % 2)
                half_copy((PF + q, q % 2))
            out_copy(NPD - 1, (NPD - 1) % 2)

        @block.vector
        def _(dve):
            V = nc.vector
            start(dve, [lru_m, hd_l, hd_qn, hd_al, bevac_done, act_ready, mod_done])
            n_small = [0]

            def chain(ins):
                n_small[0] += 1
                ins.then_inc(small, 1)
                dve.wait_ge(small, n_small[0])

            dve.wait_ge(silu, 1)
            e = tiny[:, 0:2, :].rearrange("p a b -> p (a b)")
            chain(V.tensor_scalar(e, e, 1.0, None, ALU.add))
            chain(V.reciprocal(e, e))
            chain(V.tensor_tensor(c_act[:, :], cols[:, 0:KT], e, ALU.mult))
            assert n_small[0] == SMALL_CACT
            dve.wait_ge(silu, 3)
            lam = cols[:, C_LAM:C_LAM + NT]
            e, s, s2, acc = tiny[:, 3, :], tiny[:, 4, :], tiny[:, 5, :], tiny[:, 6, :]
            chain(V.tensor_scalar(s2, e, 2.0, None, ALU.add))
            chain(V.reciprocal(s2, s2))
            chain(V.tensor_tensor(s, e, s2, ALU.mult))
            chain(V.tensor_tensor(s2, s, s, ALU.mult))
            chain(V.tensor_scalar(acc, s2, 1.0 / (2 * N_SER - 1), 1.0 / (2 * N_SER - 3), ALU.mult, ALU.add))
            for n in range(N_SER - 3, -1, -1):
                chain(V.tensor_tensor(acc, acc, s2, ALU.mult))
                chain(V.tensor_scalar(acc, acc, 1.0 / (2 * n + 1), None, ALU.add))
            chain(V.tensor_tensor(acc, acc, s, ALU.mult))
            chain(V.tensor_scalar(s, lam, -1.0, 0.0, ALU.mult, ALU.max))
            chain(V.scalar_tensor_tensor(out=acc, in0=acc, scalar=2.0, in1=s, op0=ALU.mult, op1=ALU.add))
            chain(V.tensor_scalar(c8[:, :], acc, -LRU_C, None, ALU.mult))
            assert n_small[0] == SMALL_C8
            chain(V.tensor_scalar(gqk[:, 0:1], cols[:, C_GQ:C_GQ + 1], float(HD) ** -0.5, None, ALU.mult))
            chain(V.tensor_copy(gqk[:, 1:2], cols[:, C_GQ + 1:C_GQ + 2]))

            def mod_add(b, bank, src_off):
                dve.wait_ge(ada_sum, b + 1)
                cc = b * (AB // P)
                V.tensor_tensor(mod[:, ds(cc, AB // P)], ps[:, bank, src_off:src_off + AB // P],
                                cols[:, ds(C_BADA + cc, AB // P)], ALU.add).then_inc(mod_done, 1)

            with dve.Fori(0, PRO_BLOCKS // 2) as i:
                for hb in range(2):
                    b = 2 * i + hb
                    for q in range(KT):
                        dve.wait_ge(pro_in[q % 8], 16 * (2 * b + q // 8 + 1))
                        if q == 0:
                            V.tensor_scalar(pro_acc[:, hb, :], pro_w[:, 0, :], c_act[:, 0:1], None,
                                            ALU.mult).then_inc(ada_done, 1)
                        else:
                            dve.wait_ge(ada_done, b * KT + q)
                            V.scalar_tensor_tensor(out=pro_acc[:, hb, :], in0=pro_w[:, q % 8, :],
                                                   scalar=c_act[:, q:q + 1], in1=pro_acc[:, hb, :],
                                                   op0=ALU.mult, op1=ALU.add).then_inc(ada_done, 1)
                    mod_add(b, 2, 0)
            reach(dve, mod_done, PRO_BLOCKS)
            chain(V.scalar_tensor_tensor(out=sg[:, 0, :], in0=mod[:, KT:2 * KT], scalar=1.0,
                                         in1=cols[:, C_N1:C_N1 + KT], op0=ALU.add, op1=ALU.mult))
            chain(V.memset(ada_acc[:, :], 0.0))

            def norm(which, n0):
                dve.wait_ge(rstd, 2 * which + 1)
                V.reciprocal(t3[:, 1, :], t3[:, 0, :]).then_inc(rstd, 1)
                dve.wait_ge(rstd, 2 * which + 2)
                sh = 0 if which == 0 else 3 * KT
                with dve.Fori(0, KT // 2) as i:
                    for j in range(2):
                        t = (t1, t2)[j]
                        n = 2 * i + j
                        reach(dve, act_ready, KT * which + i)
                        V.scalar_tensor_tensor(out=t[:, 0:1, :], in0=xT[:, ds(n, 1), :],
                                               scalar=sg[:, which, ds(n, 1)], in1=t3[:, 1:2, :],
                                               op0=ALU.mult, op1=ALU.mult).then_inc(nrm_t, 1)
                    for j in range(2):
                        t = (t1, t2)[j]
                        n = 2 * i + j
                        dve.wait_ge(nrm_h, n0 + n + 1)
                        m = V.scalar_tensor_tensor(out=actv[:, ds(n, 1), 1, :], in0=t[:, 0:1, :],
                                                   scalar=mod[:, ds(sh + n, 1)],
                                                   in1=actv[:, ds(n, 1), 0, :].bitcast(F32),
                                                   op0=ALU.add, op1=ALU.subtract)
                    m.then_inc(act_ready, 1)

            def lo_chunk(p, k):
                dve.wait_ge(hi_done, CH * p + k + 1)
                V.tensor_tensor(w_lo[:, k, :], raw[:, k, :], w_hi[:, k, :].bitcast(F32),
                                ALU.subtract).then_inc(lo_done, 1)

            for k in range(CH):
                lo_chunk(0, k)
            norm(0, 0)

            def ada_add(q, m, kt0):
                for a in range(2):
                    dve.wait_ge(ada_in[a], 8 * (m + 2))
                    dve.wait_ge(ada_done, PRO_ADA + m + a)
                    V.scalar_tensor_tensor(out=ada_acc[:, :], in0=ada_w[:, a, :],
                                           scalar=c_act[:, ds(kt0 + a, 1)], in1=ada_acc[:, :],
                                           op0=ALU.mult, op1=ALU.add).then_inc(ada_done, 1)

            def ada_flush(b):
                mod_add(b, 2, 256)
                chain(V.memset(ada_acc[:, :], 0.0))

            def psum_sum(dst, b0, s):
                return V.tensor_tensor(dst, pm[:, b0:b0 + 2, 0:S], half[:, :, :], ALU.add).then_inc(s, 1)

            def stage(p0, bodies, ada=None, pre=None, mid=None, post=None, dst=None, used=None):
                def body(i):
                    for j in range(2):
                        q = 2 * i + j
                        p = p0 + q
                        if ada:
                            ada_add(q, ada[0] + 2 * q, ada[1] + 2 * q)
                        if pre:
                            pre(i, j, q, p)
                        for k in range(CH):
                            lo_chunk(p + 1, k)
                            if mid:
                                mid(i, j, q, k, p)
                        if dst is not None:
                            if used:
                                dve.wait_ge(res, used(q))
                            dve.wait_ge(half_done, p + 1)
                            psum_sum(dst(q), 2 * j, evac_done)
                        if post:
                            post(i, j, q, p)
                if isinstance(bodies, list):
                    for i in bodies:
                        body(i)
                else:
                    with dve.Fori(0, bodies) as i:
                        body(i)

            stage(P_LX, [0, 1], ada=(0, 0), dst=lambda q: lx[:, 2 * q:2 * q + 2, :])

            def conv(i, j, q, p):
                for n in range(2):
                    dve.wait_ge(conv_0, 2 * q + n + 1)
                    for d in range(1, TAPS):
                        if d > 1:
                            dve.wait_ge(conv_s, 6 * q + 3 * n + d - 1)
                        V.scalar_tensor_tensor(
                            out=lru_u[:, ds(2 * q + n, 1), d:S], in0=lx[:, ds(2 * q + n, 1), 0:S - d],
                            scalar=cols[:, ds(C_CW + (TAPS - 1 - d) * NT + 2 * q + n, 1)],
                            in1=lru_u[:, ds(2 * q + n, 1), d:S], op0=ALU.mult, op1=ALU.add).then_inc(conv_s, 1)
            stage(P_LG, BW, ada=(8, 8), pre=conv, dst=lambda q: lg[:, ds(2 * q, 2), :])
            ada_flush(4)

            def gate_u(i, j, q, p):
                reach(dve, ri_sig, 4 * q + 4)
                V.tensor_tensor(lru_iu[:, ds(2 * q, 2), :], lru_iu[:, ds(2 * q, 2), :],
                                lru_u[:, ds(2 * q, 2), :], ALU.mult).then_inc(iu_done, 1)
            stage(P_Q, BW, ada=(16, 0), post=gate_u, dst=lambda q: qk[:, ds(2 * q, 2), 0, :])

            def mult2(i, j, q, p):
                dve.wait_ge(lru_t, 5 * q + 5)
                V.reciprocal(t1[:, :, :], t1[:, :, :]).then_inc(lru_m, 1)
                reach(dve, lru_m, 2 * q + 1)
                V.scalar_tensor_tensor(out=lru_r[:, ds(2 * q, 2), :], in0=lru_r[:, ds(2 * q, 2), :], scalar=-2.0,
                                       in1=t1[:, :, :], op0=ALU.mult, op1=ALU.mult).then_inc(lru_m, 1)
            stage(P_K, BW, ada=(24, 8), post=mult2, dst=lambda q: qk[:, ds(2 * q, 2), 1, :])
            ada_flush(5)

            def scan(i, j, q, p):
                dve.wait_ge(lru_q, q + 1)
                V.tensor_tensor(lru_r[:, ds(2 * q, 2), :], lru_r[:, ds(2 * q, 2), :],
                                lru_iu[:, ds(2 * q, 2), :], ALU.mult).then_inc(lru_s, 1)
                dve.wait_ge(lru_s, 4 * q + 1)
                for n in range(2):
                    V.tensor_tensor_scan(flat(lru_u, (2 * q + n) * S, S), flat(lru_a, (2 * q + n) * S, S),
                                         flat(lru_r, (2 * q + n) * S, S), 0.0, ALU.mult,
                                         ALU.add).then_inc(lru_s, 1)
                dve.wait_ge(lru_s, 4 * q + 3)
                dve.wait_ge(gelu_done, 1)
                V.tensor_tensor(t1[:, :, :], lru_u[:, ds(2 * q, 2), :], lg[:, ds(2 * q, 2), :],
                                ALU.mult).then_inc(lru_s, 1)

            def rec_lo(i, j, q, p):
                dve.wait_ge(yb_hi, q + 1)
                V.tensor_tensor(yb[:, ds(2 * q, 2), 1, :], t1[:, :, :], yb[:, ds(2 * q, 2), 0, :].bitcast(F32),
                                ALU.subtract).then_inc(yb_ready, 1)
            stage(P_V, BW, pre=scan, post=rec_lo, dst=lambda q: vT[:, ds(2 * q, 2), :])

            def head(h0):
                def pre(i, j, q, p):
                    h = i + h0
                    if j == 1:
                        dve.wait_ge(hd_r, 5 * h + 4)
                        reach(dve, hd_tail, h)
                        V.tensor_tensor(lsum[:, :], zr[:, :], wgt[:, :], ALU.add).then_inc(hd_l, 1)

                def mid(i, j, q, k, p):
                    h = i + h0
                    if j == 0 and k == 1:
                        dve.wait_ge(hd_rs, h + 1)
                        for t in range(2):
                            V.scalar_tensor_tensor(out=qn[:, t:t + 1, :], in0=qk[:, ds(h, 1), t, :],
                                                   scalar=gqk[:, t:t + 1], in1=t2[:, t:t + 1, :],
                                                   op0=ALU.mult, op1=ALU.mult).then_inc(hd_qn, 1)

                def post(i, j, q, p):
                    h = i + h0
                    if j == 1:
                        dve.wait_ge(hd_ah, h + 1)
                        V.tensor_tensor(att[:, ds(h, 1), 1, :], ps[:, 3:4, 0:S],
                                        att[:, ds(h, 1), 0, :].bitcast(F32), ALU.subtract).then_inc(hd_al, 1)
                return pre, mid, post

            pre, mid, post = head(0)
            stage(P_GA, BD, ada=(32, 0), pre=pre, mid=mid, post=post, dst=lambda q: gates[:, 0, ds(2 * q, 2), :])
            ada_flush(6)
            pre, mid, post = head(NT // 2)
            stage(P_GB, BD, ada=(48, 0), pre=pre, mid=mid, post=post, dst=lambda q: gates[:, 1, ds(2 * q, 2), :])
            ada_flush(7)

            def b_evac(i, j, q, k, p):
                if k == 1:
                    dve.wait_ge(bhalf_done, q + 1)
                    psum_sum(t1[:, :, :], 0, bevac_done)
                    reach(dve, bevac_done, q + 1)
                    dve.wait_ge(sga, 2 * q + 2)
                    V.tensor_tensor(t1[:, :, :], t1[:, :, :], gates[:, 1, ds(2 * q, 2), :],
                                    ALU.mult).then_inc(mrg, 1)

            def merge(i, j, q, p):
                dve.wait_ge(half_done, p + 1)
                psum_sum(t2[:, :, :], 2, evac_done)
                dve.wait_ge(evac_done, p + 1)
                V.tensor_tensor(t2[:, :, :], t2[:, :, :], gates[:, 0, ds(2 * q, 2), :], ALU.mult).then_inc(mrg, 1)
                dve.wait_ge(mrg, 5 * q + 2)
                V.tensor_tensor(t2[:, :, :], t2[:, :, :], t1[:, :, :], ALU.add).then_inc(mrg, 3)
                dve.wait_ge(mrg_h, q + 1)
                V.tensor_tensor(actv[:, ds(2 * q, 2), 1, :], t2[:, :, :], actv[:, ds(2 * q, 2), 0, :].bitcast(F32),
                                ALU.subtract).then_inc(act_ready, 1)
            stage(P_BR, BD, ada=(64, 0), mid=b_evac, post=merge)
            ada_flush(8)

            chain(V.memset(t2[:, :, :], 0.0))
            assert n_small[0] == SMALL_T2

            def resid(i, j, q, p):
                dve.wait_ge(evac_done, p + 1)
                for n in range(2):
                    m = V.scalar_tensor_tensor(out=xT[:, ds(2 * q + n, 1), :], in0=t1[:, n:n + 1, :],
                                               scalar=mod[:, ds(2 * KT + 2 * q + n, 1)],
                                               in1=xT[:, ds(2 * q + n, 1), :], op0=ALU.mult, op1=ALU.add)
                    m.then_inc(res, 1 + n)
            stage(P_OUT, BD, ada=(80, 0), post=resid, dst=lambda q: t1[:, :, :])
            ada_flush(9)
            reach(dve, mod_done, 10)
            chain(V.scalar_tensor_tensor(out=sg[:, 1, :], in0=mod[:, 4 * KT:5 * KT], scalar=1.0,
                                         in1=cols[:, C_N2:C_N2 + KT], op0=ALU.add, op1=ALU.mult))
            norm(1, KT)
            chain(V.memset(mlp_acc[:, :, :], 0.0))

            R0 = 3 * NPD
            RG = 4 * NPD

            def relu2(n0, e0):
                def f(i, j, q, p):
                    dve.wait_ge(evac_done, p + 1)
                    V.scalar_tensor_tensor(out=t2[:, :, :], in0=t1[:, :, :], scalar=0.0, in1=t1[:, :, :],
                                           op0=ALU.max, op1=ALU.mult).then_inc(res, 2)
                    dve.wait_ge(hid_h, e0 + q + 1)
                    V.tensor_tensor(hid[:, ds(2 * q, 2), 1, :], t2[:, :, :],
                                    hid[:, ds(2 * q, 2), 0, :].bitcast(F32), ALU.subtract).then_inc(act_ready, 1)
                return f

            def accum(i, j, q, p):
                dve.wait_ge(evac_done, p + 1)
                V.tensor_tensor(mlp_acc[:, ds(2 * q, 2), :], mlp_acc[:, ds(2 * q, 2), :], t1[:, :, :],
                                ALU.add).then_inc(res, 2)

            to_t1 = lambda q: t1[:, :, :]
            def steps(g, half):
                return lambda q: R0 + RG * g + 2 * NPD * half + 2 * q
            stage(P_MLP, BD, ada=(96, 0), post=relu2(R0, 0), dst=to_t1, used=steps(0, 0))
            ada_flush(10)
            stage(P_MLP + NPD, BD, ada=(112, 0), post=accum, dst=to_t1, used=steps(0, 1))
            mod_add(11, 2, 256)
            with dve.Fori(1, GROUPS - 1) as g:
                stage(P_MLP + 2 * NPD * g, BD, post=relu2(R0 + RG * g, NPD * g), dst=to_t1,
                      used=steps(g, 0))
                stage(P_MLP + 2 * NPD * g + NPD, BD, post=accum, dst=to_t1, used=steps(g, 1))
            stage(P_MLP + 2 * NPD * (GROUPS - 1), BD, post=relu2(R0 + RG * (GROUPS - 1), NPD * (GROUPS - 1)),
                  dst=to_t1, used=steps(GROUPS - 1, 0))

            PF = N_PANELS - NPD
            RF = R0 + RG * GROUPS - 2 * NPD
            for q in range(NPD):
                p = PF + q
                if q + 1 < NPD:
                    for k in range(CH):
                        lo_chunk(p + 1, k)
                dve.wait_ge(half_done, p + 1)
                dve.wait_ge(res, RF + 2 * q)
                psum_sum(t1[:, :, :], 2 * (q % 2), evac_done)
                dve.wait_ge(evac_done, p + 1)
                V.tensor_tensor(t1[:, :, :], t1[:, :, :], mlp_acc[:, 2 * q:2 * q + 2, :], ALU.add).then_inc(res, 1)
                dve.wait_ge(res, RF + 2 * q + 1)
                if q > 0:
                    dve.wait_ge(out_t, q)
                for n in range(2):
                    m = V.scalar_tensor_tensor(out=t2[:, n, :], in0=t1[:, n, :],
                                               scalar=mod[:, 5 * KT + 2 * q + n:5 * KT + 2 * q + n + 1],
                                               in1=xT[:, 2 * q + n, :], op0=ALU.mult, op1=ALU.add)
                m.then_inc(res, 1)

        @block.tensor
        def _(pe):
            MM = nc.tensor.matmul
            start(pe, [ri_mm, hd_ssq, hd_vt, hd_att, hd_tail])

            pe.wait_ge(consts, 6)
            pe.wait_ge(vec_in, 16 * 12)
            for g in range(3):
                nc.tensor.transpose(ps[:, 0, g * P:(g + 1) * P], vec_rows[:, g, :], ident[:, :]).then_inc(vec_t, 1)
            def sum_x(b):
                pe.wait_ge(x_sq, b + 1)
                for t in range(2):
                    m = MM(ps[:, 1, 0:S], ones[:, :], (t1, t2)[b % 2][:, t, :], start=(b == 0 and t == 0),
                           stop=(b == KT // 2 - 1 and t == 1))
                m.then_inc(ssq, 1)

            for b in range(TOK):
                pe.wait_ge(x_in[b], 16)
            for b in range(KT // 2):
                if b >= 4:
                    pe.wait_ge(x_c, b - 3)
                for t in range(2):
                    for k in range(TOK):
                        m = nc.tensor.transpose(pm[:, b % 4, t * S + k * P:t * S + (k + 1) * P],
                                                x_rows[:, k, (2 * b + t) * P:(2 * b + t + 1) * P], ident[:, :])
                m.then_inc(x_t, 1)
                if b >= 1:
                    sum_x(b - 1)
            sum_x(KT // 2 - 1)

            def ada_reduce(acc, bank, off, done, prev):
                pe.wait_ge(ada_done, done)
                reach(pe, mod_done, prev)
                for t in range(AB // P):
                    m = MM(ps[:, bank, off + t:off + t + 1], acc[:, t * P:(t + 1) * P], ones[:, 0:1],
                           start=True, stop=True)
                m.then_inc(ada_sum, 1)

            with pe.Fori(0, PRO_BLOCKS // 2) as i:
                for hb in range(2):
                    ada_reduce(pro_acc[:, hb, :], 2, 0, (2 * i + hb + 1) * KT, 2 * i + hb)

            def split_mm(bank, k, o, a, first, last):
                for hi in ((True, False) if first or not last else (False, True)):
                    if hi:
                        m = MM(pm[:, bank, :], w_hi[:, k, o:o + P], a, start=first, stop=last)
                    else:
                        m = MM(pm[:, bank, S:2 * S], w_lo[:, k, o:o + P], a[:, 0:S], start=False, stop=False,
                               skip_group_check=True)
                return m

            def panel(p, j, mov, ready=None, after=None):
                for k in range(CH):
                    if ready:
                        ready(k)
                    if k == 0:
                        reach(pe, evac_done, p - 1)
                    pe.wait_ge(lo_done, CH * p + k + 1)
                    for kk in range(KC):
                        a = mov(KC * k + kk)
                        for t in range(2):
                            m = split_mm(2 * j + t, k, kk * PAN + t * P, a, k == 0 and kk == 0,
                                         k == CH - 1 and kk == KC - 1)
                    m.then_inc(mm_done, 1)
                    if after:
                        after(k)

            def mov_of(t):
                return lambda k: t[:, k, :, :].rearrange("p a t -> p (a t)")

            def stage(p0, bodies, mov, ready=None, after=None):
                def body(i):
                    for j in range(2):
                        q = 2 * i + j
                        panel(p0 + q, j, mov, ready, (lambda k: after(i, j, q, k)) if after else None)
                if isinstance(bodies, list):
                    for i in bodies:
                        body(i)
                else:
                    with pe.Fori(0, bodies) as i:
                        body(i)

            def tiles_ready(base):
                return lambda k: reach(pe, act_ready, base + (k + 1) * KC // 2)

            h_mov = mov_of(actv)
            stage(P_LX, [0, 1], h_mov, ready=tiles_ready(0))
            stage(P_LG, BW, h_mov)
            ada_reduce(ada_acc, 2, 256, PRO_ADA + 16, 0)

            def ri(i, j, q, k):
                if k != 1:
                    return
                pe.wait_ge(lru_w_in, 32 * (q + 1))
                reach(pe, ri_sig, 4 * q)
                pe.wait_ge(conv_s, 6 * NPW)
                for n in range(2):
                    for g in range(2):
                        m = MM(ps[:, g, n * S:(n + 1) * S], lru_w[:, 2 * g + n, :], flat(lru_u, (2 * q + n) * S, S),
                               start=True, stop=True)
                m.then_inc(ri_mm, 1)
            stage(P_Q, BW, h_mov, after=ri)
            stage(P_K, BW, h_mov)
            ada_reduce(ada_acc, 2, 256, PRO_ADA + 32, 5)
            stage(P_V, BW, h_mov)

            def head(h0, blocks):
                def f(i, j, q, k):
                    h = i + h0
                    if j == 0 and k == 0:
                        reach(pe, mod_done, blocks)
                        pe.wait_ge(hd_sq, h + 1)
                        MM(ps[:, 0, :], ones[:, :], t1[:, :, :].rearrange("p a t -> p (a t)"),
                           start=True, stop=True).then_inc(hd_ssq, 1)
                        pe.wait_ge(hd_vc, h + 1)
                        for b in range(TOK):
                            m = nc.tensor.transpose(ps[:, 2, b * P:(b + 1) * P], v_col[:, b * P:(b + 1) * P],
                                                    ident[:, :])
                        m.then_inc(hd_vt, 1)
                    if j == 0 and k == 3:
                        reach(pe, hd_qn, 2 * h + 2)
                        reach(pe, hd_e, h)
                        MM(ps[:, 1, 0:S], qn[:, 1, 0:P], qn[:, 0, :], start=True, stop=True)
                        MM(ps[:, 1, S:S + P], qn[:, 1, P:S], qn[:, 0, P:S], start=False, stop=True,
                           skip_group_check=True).then_inc(hd_z, 1)
                    if j == 1 and k == 1:
                        pe.wait_ge(hd_lm, h + 1)
                        MM(ps[:, 1, 0:S], neg_tri[:, :], lsum[:, 0:S], start=False, stop=True, skip_group_check=True)
                        MM(ps[:, 1, P:S], neg_one[:, :], lsum[:, S:S + P], start=False, stop=True,
                           skip_group_check=True)
                        MM(ps[:, 1, S:S + P], neg_tri[:, :], lsum[:, S:S + P], start=False, stop=True,
                           skip_group_check=True).then_inc(hd_tail, 1)
                    if j == 1 and k == 3:
                        pe.wait_ge(hd_w, h + 1)
                        pe.wait_ge(hd_vr, h + 1)
                        reach(pe, hd_al, h)
                        MM(ps[:, 3, 0:S], v_row[:, 0, :], wgt[:, 0:S], start=True, stop=True)
                        MM(ps[:, 3, P:S], v_row[:, 1, :], wgt[:, S:S + P], start=False, stop=True,
                           skip_group_check=True).then_inc(hd_att, 1)
                return f

            stage(P_GA, BD, h_mov, after=head(0, 6))
            ada_reduce(ada_acc, 2, 256, PRO_ADA + 48, 6)
            stage(P_GB, BD, h_mov, after=head(NT // 2, 7))
            ada_reduce(ada_acc, 2, 256, PRO_ADA + 64, 7)

            with pe.Fori(0, BD) as i:
                for j in range(2):
                    q = 2 * i + j
                    p = P_BR + q
                    for k in range(CH):
                        if k == 0:
                            pe.wait_ge(yb_ready, NPW)
                            pe.wait_ge(evac_done, P_BR - 1)
                            reach(pe, bevac_done, q)
                        if k == 2:
                            reach(pe, hd_al, NT)
                            pe.wait_ge(evac_done, p)
                        pe.wait_ge(lo_done, CH * p + k + 1)
                        mv = mov_of(yb if k < 2 else att)
                        b0 = 0 if k < 2 else 2
                        for kk in range(KC):
                            a = mv(KC * (k % 2) + kk)
                            for t in range(2):
                                m = split_mm(b0 + t, k, kk * PAN + t * P, a, k % 2 == 0 and kk == 0,
                                             k % 2 == 1 and kk == KC - 1)
                        m.then_inc(mm_done, 1)
            ada_reduce(ada_acc, 2, 256, PRO_ADA + 80, 8)

            pe.wait_ge(small, SMALL_T2)
            MM(ps[:, 0, 0:S], ones[:, :], t2[:, 0, :], start=True, stop=True)

            def sum_x2(i, j, q, k):
                if k != 1:
                    return
                reach(pe, sq2, q)
                for t in range(2):
                    m = MM(ps[:, 0, 0:S], ones[:, :], t2[:, t, :], start=False, stop=True, skip_group_check=True)
                m.then_inc(ssq2, 1)

            rdy = tiles_ready(KT // 2)

            def out_ready(k):
                rdy(k)
                if k == 0:
                    reach(pe, bevac_done, NPD)
            stage(P_OUT, BD, h_mov, ready=out_ready, after=sum_x2)
            reach(pe, sq2, NPD)
            for t in range(2):
                m = MM(ps[:, 0, 0:S], ones[:, :], t2[:, t, :], start=False, stop=True, skip_group_check=True)
            m.then_inc(ssq2, 1)
            ada_reduce(ada_acc, 2, 256, PRO_ADA + 96, 9)

            AR = KT
            stage(P_MLP, BD, h_mov, ready=tiles_ready(AR))
            ada_reduce(ada_acc, 2, 256, PRO_ADA + 112, 10)
            hid_mov = mov_of(hid)
            stage(P_MLP + NPD, BD, hid_mov, ready=tiles_ready(AR + KT // 2))
            ada_reduce(ada_acc, 2, 256, PRO_ADA + 128, 11)
            with pe.Fori(1, GROUPS - 1) as g:
                stage(P_MLP + 2 * NPD * g, BD, h_mov)
                base = AR + KT // 2 + (KT // 2) * g
                stage(P_MLP + 2 * NPD * g + NPD, BD, hid_mov,
                      ready=lambda k: reach(pe, act_ready, base + (k + 1) * KC // 2))
            g = GROUPS - 1
            stage(P_MLP + 2 * NPD * g, BD, h_mov)
            base = AR + KT // 2 + (KT // 2) * g
            PF = N_PANELS - NPD
            RF = 3 * NPD + 4 * NPD * GROUPS - 2 * NPD

            def out_rows_of(q):
                pe.wait_ge(res, RF + 2 * q + 2)
                reach(pe, out_c, q)
                for b in range(TOK):
                    for t in range(2):
                        m = nc.tensor.transpose(ps[:, 1, b * PAN + t * P:b * PAN + (t + 1) * P],
                                                t2[:, t, b * P:(b + 1) * P], ident[:, :])
                m.then_inc(out_t, 1)

            for q in range(NPD):
                panel(PF + q, q % 2, hid_mov, ready=tiles_ready(base),
                      after=lambda k: out_rows_of(q - 1) if k == 1 and q > 0 else None)
            out_rows_of(NPD - 1)


_INS = ['x', 'c', 'w_ada', 'b_ada', 'norm1_g', 'w_in', 'b_in', 'q_norm_g', 'k_norm_g', 'conv_w', 'conv_b',
        'w_rg', 'b_rg', 'w_ig', 'b_ig', 'lru_lambda', 'w_branch_a', 'w_branch_b', 'w_out', 'norm2_g',
        'w_mlp_in', 'w_mlp_out']


def kernel(**inputs):
    import numpy as _np
    import concourse.bacc as _bacc
    from concourse import mybir as _mybir
    from concourse.bass_utils import run_bass_kernel_spmd as _run

    nc = _bacc.Bacc("TRN2", target_bir_lowering=False, num_devices=1)
    arrays, args = {}, []
    for name in _INS:
        a = _np.ascontiguousarray(inputs[name])
        arrays[f"in_{name}_dram"] = a
        args.append(nc.dram_tensor(f"in_{name}_dram", a.shape, _mybir.dt.from_np(a.dtype), kind="ExternalInput").ap())
    shape = inputs["x"].shape
    args.append(nc.dram_tensor("out_dram", shape, _mybir.dt.float32, kind="ExternalOutput").ap())
    hybrid_block(nc, *args)
    r = _run(nc, [arrays], core_ids=[0])
    return r.results[0]["out_dram"]
```

```python
import math
from contextlib import ExitStack

import concourse.bass as bass
from concourse import mybir

F32 = mybir.dt.float32
F32R = mybir.dt.float32r
ACT = mybir.ActivationFunctionType
ALU = mybir.AluOpType
ds = bass.ds

P = 128
EPS = 1e-6
LRU_C = 8.0


def hybrid_block(nc, x, c, w_ada, b_ada, norm1_g, w_in, b_in, q_norm_g, k_norm_g, conv_w, conv_b,
                 w_rg, b_rg, w_ig, b_ig, lru_lambda, w_branch_a, w_branch_b, w_out, norm2_g,
                 w_mlp_in, w_mlp_out, out):
    S, D = x.shape[1], x.shape[2]
    W = conv_w.shape[2]
    HD = q_norm_g.shape[1]
    DFF = w_mlp_in.shape[2]
    TAPS = conv_w.shape[1]
    KT = D // P
    NT = W // P
    TOK = S // P
    PAN = 256
    CH = 4
    KC = KT // CH
    AB = 1024
    NMOD = w_ada.shape[2]
    assert S == 256 and HD == P and PAN == 2 * P and KT == 16 and NT == 8 and TAPS == 4

    NPW = W // PAN
    NPD = D // PAN
    P_LX, P_LG = 0, NPW
    P_Q, P_K, P_V = 2 * NPW, 3 * NPW, 4 * NPW
    P_GA = 5 * NPW
    P_GB = P_GA + NPD
    P_BR = P_GB + NPD
    P_OUT = P_BR + NPD
    P_MLP = P_OUT + NPD
    GROUPS = DFF // D
    N_PANELS = P_MLP + GROUPS * 2 * NPD
    C_Q, C_K, C_V, C_LX, C_LG, C_GA, C_GB = 0, W, 2 * W, 3 * W, 4 * W, 5 * W, 5 * W + D
    PRO_BLOCKS = 2 * D // AB
    PE_Q = [3, 7, 12]
    DVE_Q = [q for q in range(KT) if q not in PE_Q]
    PRO_ADA = PRO_BLOCKS * len(DVE_Q)
    PRO_ORDER = (0, 2, 1, 3)
    ADA_ORDER = {PRO_BLOCKS + n: b for n, b in enumerate((4, 5, 8, 9, 6, 7, 10, 11))}

    w_ada_v = w_ada[0]
    w_in_v = w_in[0].rearrange("(t p) n -> p t n", p=P)
    w_ba_v = w_branch_a[0].rearrange("(t p) n -> p t n", p=P)
    w_bb_v = w_branch_b[0].rearrange("(t p) n -> p t n", p=P)
    w_out_v = w_out[0].rearrange("(t p) n -> p t n", p=P)
    w_mi_v = w_mlp_in[0].rearrange("(t p) n -> p t n", p=P)
    w_mo_v = w_mlp_out[0].rearrange("(t p) n -> p t n", p=P)
    w_rg_v = w_rg[0].rearrange("n d e -> d n e")
    w_ig_v = w_ig[0].rearrange("n d e -> d n e")
    out_v = out[0].rearrange("(b p) n -> p b n", p=P)

    with ExitStack() as ctx:
        base = (nc.sbuf_base + 31) // 32 * 32
        top = [base]

        def at(name, shape, offset, dt=F32):
            return nc.alloc_sbuf_tensor_at(name, [P] + shape, dt, offset=offset)

        def new(name, shape, dt=F32):
            o = top[0]
            top[0] += (4 * math.prod(shape) + 31) // 32 * 32
            return at(name, shape, o, dt)

        def region(nbytes):
            o = top[0]
            top[0] += nbytes
            return o

        TILE = 4 * S
        raw = new("raw_w", [CH, KC * PAN])
        w_hi = new("w_hi", [CH, KC * PAN], F32R)
        w_lo = new("w_lo", [CH, KC * PAN], F32R)
        ada_w = new("ada_w", [2, AB])
        r_acc = region(4 * AB)
        out_rows = new("out_rows", [2, TOK, PAN])
        ada_accs = [at("ada_acc_even", [AB], r_acc), at("ada_acc_odd", [AB], r_acc + 4 * AB)]
        actv = new("actv", [KT, 2, S], F32R)
        xT = new("xT", [KT, S])
        r_mix = region(4 * NT * TILE)
        r_lg = r_mix + NT * TILE
        r_qk = r_mix + 2 * NT * TILE
        lx = at("lru_x", [NT, S], r_mix)
        lg = at("lru_gate", [NT, S], r_lg)
        yb = at("yb_in", [NT, 2, S], r_mix, F32R)
        qk = at("qk", [NT, 2, S], r_qk)
        att = at("att", [NT, 2, S], r_qk, F32R)
        hid = at("hidden", [KT, 2, S], r_mix, F32R)
        pro_w = at("pro_w", [8, AB], r_mix)
        vT = new("vT", [NT, S])
        r_gate = region(2 * KT * TILE)
        gates = at("gates", [2, KT, S], r_gate)
        x_rows = at("x_rows", [TOK, D], r_gate)
        vec_rows = at("vec_rows", [3, P], r_gate + 4 * TOK * D)
        c_rows = at("c_rows", [P], r_gate + 4 * TOK * D + 2048 + 8 * AB)
        pro_acc = at("pro_acc", [2, AB], r_gate + 4 * TOK * D + 2048)
        lru_u = at("lru_u", [NT, S], r_gate)
        lru_r = at("lru_r", [NT, S], r_gate + NT * TILE)
        lru_iu = at("lru_iu", [NT, S], r_gate + 2 * NT * TILE)
        lru_a = at("lru_a", [NT, S], r_gate + 3 * NT * TILE)
        mlp_acc = at("mlp_acc", [KT, S], r_gate)
        half = new("half", [2, S])
        t1 = new("t1", [2, S])
        t2 = new("t2", [2, S])
        t3 = new("t3", [2, S])
        lru_w = new("lru_w", [4, P])
        ident = new("ident", [P])
        ones = new("ones", [P])
        neg_tri = new("neg_tri", [P])
        neg_one = new("neg_one", [P])
        cols = new("cols", [3 * P])
        c_act = new("c_act", [KT])
        mod = new("mod", [NMOD // P])
        sg = new("sg", [2, KT])
        c8 = new("c8", [NT])
        gqk = new("gqk", [2])
        eps = new("eps", [1])
        tiny = new("tiny", [8, NT])
        qn = new("qn", [2, S])
        lsum = new("lsum", [3 * P])
        wgt = new("wgt", [3 * P])
        v_col = new("v_col", [S])
        v_row = new("v_row", [TOK, P])
        zr = new("zr", [3 * P])
        assert top[0] <= nc.sbuf_usable_end, top[0] - nc.sbuf_usable_end
        ctx.enter_context(nc.sbuf_tensor("arena", [P, (top[0] - base) // 4 + 8], F32))

        pm = ctx.enter_context(nc.psum_tensor("panel_sums", [P, 4, 512], F32))
        ps = ctx.enter_context(nc.psum_tensor("side_sums", [P, 4, 512], F32))

        C_C, C_BADA, C_N1 = 0, KT, KT + NMOD // P
        C_BIN, C_N2, C_CW, C_CB = P, P + 72, P + 88, P + 120
        C_BRG, C_BIG, C_LAM, C_GQ = 2 * P, 2 * P + NT, 2 * P + 2 * NT, 2 * P + 3 * NT
        assert C_N1 + KT == P and NMOD // P == 96 and w_in.shape[2] // P == 72

        def sem(name):
            return ctx.enter_context(nc.semaphore(name))

        started = []

        def sem1(name):
            started.append(sem(name))
            return started[-1]

        raw_in = [sem(f"raw_in{s}") for s in range(CH)]
        ada_in = [sem(f"ada_in{s}") for s in range(2)]
        pro_in = [sem(f"pro_in{s}") for s in range(8)]
        x_in = [sem(f"x_in{b}") for b in range(TOK)]
        vec_zero = sem("vec_zero")
        c_in = sem("c_in")
        c_t = sem("c_t")
        vec_in = sem("vec_in")
        consts = sem("consts")
        fills = sem("fills")
        sg_done = sem("sg_done")
        hi_done = sem("hi_done")
        lo_done = sem("lo_done")
        mm_done = sem("mm_done")
        half_done = sem("half_done")
        evac_done = sem("evac_done")
        bhalf_done = sem("bhalf_done")
        bevac_done = sem1("bevac_done")
        ada_done = sem("ada_done")
        ada_sum = sem("ada_sum")
        mod_done = sem1("mod_done")
        act_ready = sem("act_ready")
        vec_t = sem("vec_t")
        vec_c = sem("vec_c")
        x_t = sem("x_t")
        x_c = sem("x_c")
        x_sq = sem("x_sq")
        ssq = sem("ssq")
        rstd = sem("rstd")
        nrm_t = sem("nrm_t")
        nrm_h = sem("nrm_h")
        silu = sem("silu")
        small = sem("small")
        conv_0 = sem("conv_0")
        conv_s = sem("conv_s")
        gelu_done = sem("gelu_done")
        lru_w_in = sem("lru_w_in")
        ri_mm = sem1("ri_mm")
        ri_sig = sem1("ri_sig")
        lru_t = sem("lru_t")
        lru_m = sem1("lru_m")
        lru_q = sem("lru_q")
        lru_s = sem("lru_s")
        yb_hi = sem("yb_hi")
        yb_ready = sem("yb_ready")
        hd_sq = sem("hd_sq")
        hd_ssq = sem1("hd_ssq")
        hd_ln = sem("hd_ln")
        hd_rs = sem("hd_rs")
        hd_qn = sem1("hd_qn")
        hd_vc = sem("hd_vc")
        hd_vt = sem1("hd_vt")
        hd_vr = sem("hd_vr")
        hd_z = sem("hd_z")
        hd_r = sem("hd_r")
        hd_l = sem1("hd_l")
        hd_lm = sem("hd_lm")
        hd_tail = sem1("hd_tail")
        hd_e = sem1("hd_e")
        hd_w = sem("hd_w")
        hd_att = sem1("hd_att")
        hd_ah = sem("hd_ah")
        hd_al = sem1("hd_al")
        sga = sem("sga")
        mrg = sem("mrg")
        mrg_b = sem("mrg_b")
        mrg_h = sem("mrg_h")
        res = sem("res")
        acc_zero = sem("acc_zero")
        zeros = sem("zeros")
        pro_mm = sem("pro_mm")
        sq2 = sem1("sq2")
        ssq2 = sem1("ssq2")
        hid_h = sem("hid_h")
        out_t = sem("out_t")
        out_c = sem("out_c")
        act_passed, pool_passed = sem("act_passed"), sem("pool_passed")
        out_d = [sem(f"out_d{b}") for b in range(2)]

        def reach(eng, s, v):
            if isinstance(v, int) and v <= 0:
                return
            eng.wait_ge(s, v + 1 if s in started else v)

        def start(eng, sems):
            for s in sems:
                eng.sem_inc(s, 1)

        def passed(eng, s):
            eng.sem_inc(s, 1)

        def flat(t, off, n):
            v = t[:]
            if len(v.shape) == 3:
                v = v.rearrange("p a b -> p (a b)")
            elif len(v.shape) == 4:
                v = v.rearrange("p a b c -> p (a b c)")
            return v[:, ds(off, n)]

        BW, BD = NPW // 2, NPD // 2

        N_SER = 9
        SMALL_CACT = 2 + 3
        SMALL_C8 = SMALL_CACT + 4 + 1 + 2 * (N_SER - 2) + 4
        SMALL_GQK = SMALL_C8 + 2
        A_FIRST = {}
        for n, name in enumerate(("LX", "LG", "Q", "V", "GA1", "GA2", "GB1", "GB2", "BR1", "BR2", "OUT1",
                                  "OUT2", "MI1", "MI2", "MO1", "MO2")):
            A_FIRST[name] = n * 2 * NPW

        def ada_of(name, first=0):
            m = A_FIRST[name]
            return m - 2 * first, PRO_BLOCKS + m // KT, m % KT - 2 * first

        block = ctx.enter_context(nc.Block())

        @block.sync
        def _(sp):
            def pro_load(n, q):
                if (n, q) >= (0, 8):
                    last, m = (q - 8, n) if q >= 8 else (q + 8, n - 1)
                    if last in PE_Q:
                        sp.wait_ge(pro_mm, m * len(PE_Q) + PE_Q.index(last) + 1)
                    else:
                        sp.wait_ge(ada_done, m * len(DVE_Q) + DVE_Q.index(last) + 1)
                col = PRO_ORDER[n] * AB
                sp.dma_start(pro_w[:, q % 8, :], w_ada_v[q * P:(q + 1) * P, col:col + AB]).then_inc(pro_in[q % 8], 16)

            def load(p, k, view, t0, nt, col):
                if not isinstance(col, int):
                    col = sp.snap(col)
                src = view[:, ds(t0, nt), ds(col, PAN)] if not isinstance(t0, int) else view[:, t0:t0 + nt, ds(col, PAN)]
                reach(sp, lo_done, CH * (p - 1) + k + 1)
                sp.dma_start(raw[:, k, :].rearrange("p (t n) -> p t n", n=PAN), src).then_inc(raw_in[k], 16)

            def stage(p0, bodies, view, c0):
                with sp.Fori(0, bodies) as i:
                    for j in range(2):
                        for k in range(CH):
                            load(p0 + 2 * i + j, k, view, KC * k, KC, c0 + PAN * (2 * i + j))

            for n in range(PRO_BLOCKS):
                for q in range(KT):
                    pro_load(n, q)
                if n == 0:
                    for b in range(TOK):
                        sp.dma_start(x_rows[:, b, :], x[0, b * P:(b + 1) * P, :]).then_inc(x_in[b], 16)
                if n == 1:
                    for k in range(2):
                        load(0, k, w_in_v, KC * k, KC, C_LX)
            for j in range(NPW):
                for k in range(2 if j == 0 else 0, CH):
                    load(j, k, w_in_v, KC * k, KC, C_LX + PAN * j)
            stage(P_LG, BW, w_in_v, C_LG)
            with sp.Fori(0, BW) as i:
                for j in range(2):
                    n = sp.snap(2 * (2 * i + j))
                    for k in range(CH):
                        load(P_Q + 2 * i + j, k, w_in_v, KC * k, KC, C_Q + PAN * (2 * i + j))
                    src_r, src_i = w_rg_v[:, ds(n, 2), :], w_ig_v[:, ds(n, 2), :]
                    reach(sp, ri_mm, 2 * i + j)
                    sp.dma_start(lru_w[:, 0:2, :], src_r).then_inc(lru_w_in, 16)
                    sp.dma_start(lru_w[:, 2:4, :], src_i).then_inc(lru_w_in, 16)
            stage(P_K, BW, w_in_v, C_K)
            stage(P_V, BW, w_in_v, C_V)
            stage(P_GA, BD, w_in_v, C_GA)
            stage(P_GB, BD, w_in_v, C_GB)
            with sp.Fori(0, BD) as i:
                for j in range(2):
                    for k in range(CH):
                        view = w_bb_v if k < 2 else w_ba_v
                        load(P_BR + 2 * i + j, k, view, KC * (k % 2), KC, PAN * (2 * i + j))
            stage(P_OUT, BD, w_out_v, 0)
            def mlp_in(g):
                with sp.Fori(0, BD) as i:
                    for j in range(2):
                        for k in range(CH):
                            load(P_MLP + 2 * NPD * g + 2 * i + j, k, w_mi_v, KC * k, KC,
                                 D * g + PAN * (2 * i + j))

            with sp.Fori(0, GROUPS - 1) as g:
                mlp_in(g)
                with sp.Fori(0, BD) as i:
                    for j in range(2):
                        for k in range(CH):
                            load(P_MLP + 2 * NPD * g + NPD + 2 * i + j, k, w_mo_v, sp.snap(KT * g + KC * k), KC,
                                 PAN * (2 * i + j))
            mlp_in(GROUPS - 1)
            LAG = 3
            for q in range(NPD + LAG):
                if q < NPD:
                    for k in range(CH):
                        load(N_PANELS - NPD + q, k, w_mo_v, KT * (GROUPS - 1) + KC * k, KC, PAN * q)
                if q >= LAG:
                    r = q - LAG
                    sp.wait_ge(out_c, r + 1)
                    sp.dma_start(out_v[:, :, PAN * r:PAN * (r + 1)], out_rows[:, r % 2, :, :]).then_inc(out_d[r % 2], 16)
            for b in range(2):
                sp.wait_ge(out_d[b], 16 * BD)

        @block.gpsimd
        def _(pool):
            nc.gpsimd.memset(ident[:, :], 0.0).then_inc(consts, 1)
            pool.wait_ge(consts, 1)
            nc.gpsimd.affine_select(out=ident[:, :], in_=ident[:, :], compare_op=ALU.not_equal, fill=1.0, base=0,
                                    pattern=[[-1, P]], channel_multiplier=1).then_inc(consts, 1)
            pool.wait_ge(fills, 3)
            nc.gpsimd.affine_select(out=neg_tri[:, :], in_=neg_one[:, :], compare_op=ALU.is_ge, fill=0.0, base=0,
                                    pattern=[[-1, P]], channel_multiplier=1).then_inc(consts, 1)

            def diag(t):
                return t[:, :].rearrange("p (a b) -> p a b", b=P)[:, 0:3:2, :]

            with pool.Fori(0, NT) as h:
                reach(pool, hd_l, h + 1)
                passed(pool, pool_passed)
                nc.gpsimd.affine_select(out=diag(lsum), in_=diag(lsum), compare_op=ALU.is_gt, fill=0.0, base=0,
                                        pattern=[[0, 2], [1, P]], channel_multiplier=-1).then_inc(hd_lm, 1)
                reach(pool, hd_e, h + 1)
                passed(pool, pool_passed)
                nc.gpsimd.affine_select(out=diag(wgt), in_=diag(wgt), compare_op=ALU.is_gt, fill=0.0, base=0,
                                        pattern=[[0, 2], [1, P]], channel_multiplier=-1).then_inc(hd_w, 1)

            with pool.Fori(0, NPD) as q:
                reach(pool, bevac_done, q + 1)
                pool.wait_ge(sga, 2 * q + 1)
                passed(pool, pool_passed)
                nc.gpsimd.tensor_tensor(t1[:, :, :], t1[:, :, :], gates[:, 1, ds(2 * q, 2), :],
                                        ALU.mult).then_inc(mrg_b, 1)
            pool.wait_ge(mrg, 2 * NPD)
            nc.gpsimd.memset(mlp_acc[:, :, :], 0.0).then_inc(acc_zero, 1)

        @block.scalar
        def _(act):
            A = nc.scalar.activation
            start(act, [ri_sig, hd_e, sq2])

            act.preload_act_table(ACT.Exp)
            act.dma_start(c_rows[0:KT, :], c.rearrange("a (t p) -> (a t) p", p=P)).then_inc(c_in, 16)
            act.wait_ge(c_t, 1)
            A(tiny[:, 0:2, :].rearrange("p a b -> p (a b)"), ps[:, 3, 0:KT], ACT.Exp, scale=-1.0).then_inc(silu, 1)
            act.wait_ge(vec_zero, 1)

            def rms(sums):
                A(t3[:, 0, :], sums, ACT.Sqrt, scale=1.0 / D, bias=eps[:, 0:1]).then_inc(rstd, 1)

            def rows(v, g, r):
                n = 1
                for s in v.shape:
                    n *= s
                n //= P
                while len(v.shape) > 2:
                    v = v.rearrange("a b c -> (a b) c")
                act.dma_start(vec_rows[r:r + n, g, :], v.rearrange("a (t p) -> (a t) p", p=P)).then_inc(vec_in, 16)

            rows(b_ada, 0, C_BADA)
            rows(norm1_g, 0, C_N1)
            rows(b_in, 1, 0)
            rows(norm2_g, 1, C_N2 - P)
            rows(conv_w, 1, C_CW - P)
            rows(conv_b, 1, C_CB - P)
            rows(b_rg, 2, 0)
            rows(b_ig, 2, NT)
            rows(lru_lambda, 2, 2 * NT)
            rows(q_norm_g, 2, 3 * NT)
            rows(k_norm_g, 2, 3 * NT + 1)
            act.wait_ge(vec_t, 3)
            A(cols[:, :], ps[:, 0, 0:3 * P], ACT.Copy).then_inc(vec_c, 1)
            act.wait_ge(vec_c, 1)
            A(tiny[:, 2, :], cols[:, C_LAM:C_LAM + NT], ACT.Abs).then_inc(silu, 1)
            act.wait_ge(silu, 2)
            A(tiny[:, 3, :], tiny[:, 2, :], ACT.Exp, scale=-1.0).then_inc(silu, 1)
            for b in range(KT // 2):
                act.wait_ge(x_t, b + 1)
                A(xT[:, 2 * b:2 * b + 2, :], pm[:, b % 4, :].rearrange("p (a t) -> p a t", a=2),
                  ACT.Copy).then_inc(x_c, 1)
                if b >= 2:
                    act.wait_ge(ssq, b - 1)
                act.wait_ge(x_c, b + 1)
                A((t1, t2)[b % 2][:, :, :], xT[:, 2 * b:2 * b + 2, :], ACT.Square).then_inc(x_sq, 1)
            act.wait_ge(ssq, KT // 2)
            rms(ps[:, 1, 0:S])

            def hi_chunk(p, k):
                act.wait_ge(raw_in[k], 16 * (p + 1))
                reach(act, mm_done, CH * (p - 1) + k + 1)
                A(w_hi[:, k, :], raw[:, k, :], ACT.Copy).then_inc(hi_done, 1)

            def norm_hi(which, n):
                act.wait_ge(nrm_t, KT * which + n + 1)
                sh = 3 * KT * which + n
                A(actv[:, n, 0, :], (t1, t2)[n % 4 // 2][:, n % 2, :], ACT.Identity,
                  bias=mod[:, sh:sh + 1]).then_inc(nrm_h, 1)

            def half_copy(p, bias_col=None):
                b0 = 2 * (p[1] % 2)
                pp = p[0]
                if bias_col is None:
                    reach(act, evac_done, pp)
                    act.wait_ge(mm_done, CH * pp + CH)
                    A(half[:, :, :], pm[:, b0:b0 + 2, S:2 * S], ACT.Copy).then_inc(half_done, 1)
                else:
                    for t in range(2):
                        if t == 0:
                            reach(act, evac_done, pp)
                            act.wait_ge(mm_done, CH * pp + CH)
                            passed(act, act_passed)
                        m = A(half[:, t, :], pm[:, b0 + t, S:2 * S], ACT.Identity,
                              bias=cols[:, ds(C_BIN + bias_col + t, 1)])
                    m.then_inc(half_done, 1)

            def ada_load(a, m, blk, kt0):
                src = w_ada_v[ds(act.snap((kt0 + a) * P) if not isinstance(kt0, int) else (kt0 + a) * P, P),
                              ADA_ORDER[blk] * AB:(ADA_ORDER[blk] + 1) * AB]
                reach(act, ada_done, PRO_ADA + m + a - 1)
                act.dma_start(ada_w[:, a, :], src).then_inc(ada_in[a], 16)

            def stage(p0, bodies, ada=None, pre=None, mid=None, post=None, bias=None, evac=True):
                def body(i):
                    for j in range(2):
                        q = 2 * i + j
                        p = p0 + q
                        if ada:
                            ada_load(0, ada[0] + 2 * q, ada[1], ada[2] + 2 * q)
                        if pre:
                            pre(i, j, q)
                        for k in range(CH):
                            if k == CH - 1 and evac:
                                half_copy((p, j), None if bias is None else bias + 2 * q)
                            hi_chunk(p + 1, k)
                            if ada and k == 0:
                                ada_load(1, ada[0] + 2 * q, ada[1], ada[2] + 2 * q)
                            if mid:
                                mid(i, j, q, k, p)
                        if post:
                            post(i, j, q)
                if isinstance(bodies, list):
                    for i in bodies:
                        body(i)
                else:
                    with act.Fori(*bodies) as i:
                        body(i)

            for n in range(KT // 2):
                norm_hi(0, n)
            for k in range(CH):
                hi_chunk(0, k)
            for n in range(KT // 2, KT):
                norm_hi(0, n)
            HALF1, HALF2 = (0, BD // 2), (BD // 2, BD)
            T_LX, T_LG, T_GA, T_GB = C_LX // P, C_LG // P, C_GA // P, C_GB // P
            stage(P_LX, [0, 1], ada=ada_of("LX"), bias=T_LX)

            def conv0(i, j, q):
                for n in range(2):
                    act.wait_ge(evac_done, NPW)
                    A(lru_u[:, ds(2 * q + n, 1), :], lx[:, ds(2 * q + n, 1), :], ACT.Identity,
                      scale=cols[:, ds(C_CW + (TAPS - 1) * NT + 2 * q + n, 1)],
                      bias=cols[:, ds(C_CB + 2 * q + n, 1)]).then_inc(conv_0, 1)
            stage(P_LG, (0, BW), ada=ada_of("LG"), pre=conv0, bias=T_LG)
            act.wait_ge(evac_done, P_Q)
            A(lg[:, :, :], lg[:, :, :], ACT.Gelu_apprx_tanh).then_inc(gelu_done, 1)

            def sigm(i, j, q, k, p):
                if k != 2:
                    return
                for g, dst, b in ((0, lru_r, C_BRG), (1, lru_iu, C_BIG)):
                    for n in range(2):
                        reach(act, ri_mm, q + 1)
                        passed(act, act_passed)
                        A(dst[:, ds(2 * q + n, 1), :], ps[:, g:g + 1, n * S:(n + 1) * S], ACT.Sigmoid,
                          bias=cols[:, ds(b + 2 * q + n, 1)]).then_inc(ri_sig, 1)
            act.preload_act_table(ACT.Sigmoid)
            stage(P_Q, (0, BW), ada=ada_of("Q"), mid=sigm, bias=C_Q // P)

            def decay(i, j, q):
                tb = (t1, t2)[j]
                reach(act, lru_m, 2 * q - 2)
                act.wait_ge(small, SMALL_C8)
                reach(act, ri_sig, 4 * NPW)
                passed(act, act_passed)
                for n in range(2):
                    A(lru_a[:, ds(2 * q + n, 1), :], lru_r[:, ds(2 * q + n, 1), :], ACT.Exp,
                      scale=c8[:, ds(2 * q + n, 1)]).then_inc(lru_t, 1)
                act.wait_ge(lru_t, 5 * q + 2)
                passed(act, act_passed)
                for n in range(2):
                    A(lru_r[:, ds(2 * q + n, 1), :], lru_r[:, ds(2 * q + n, 1), :], ACT.Tanh,
                      scale=c8[:, ds(2 * q + n, 1)]).then_inc(lru_t, 1)
                act.wait_ge(lru_t, 5 * q + 4)
                passed(act, act_passed)
                A(tb[:, :, :], lru_r[:, ds(2 * q, 2), :], ACT.Identity, scale=-1.0, bias=1.0).then_inc(lru_t, 1)
            act.preload_act_table_set("exp_and_others")
            stage(P_K, [0, 1], pre=decay, bias=C_K // P)

            def mult(i, j, q):
                reach(act, lru_m, 2 * NPW)
                A(lru_r[:, ds(2 * q, 2), :], lru_r[:, ds(2 * q, 2), :], ACT.Sqrt).then_inc(lru_q, 1)

            def rec_hi(i, j, q):
                act.wait_ge(lru_s, 4 * q + 4)
                passed(act, act_passed)
                A(yb[:, ds(2 * q, 2), 0, :], t1[:, :, :], ACT.Copy).then_inc(yb_hi, 1)
            act.preload_act_table(ACT.Sqrt)
            stage(P_V, (0, BW), ada=ada_of("V"), pre=mult, post=rec_hi, bias=C_V // P)

            def head(h0):
                def pre(i, j, q):
                    h = i + h0
                    if j == 0:
                        reach(act, hd_ssq, h)
                        act.wait_ge(evac_done, P_V)
                        passed(act, act_passed)
                        A(t3[:, :, :], qk[:, ds(h, 1), :, :], ACT.Square).then_inc(hd_sq, 1)
                        reach(act, hd_vt, h)
                        act.wait_ge(evac_done, P_V + 1 + h)
                        passed(act, act_passed)
                        A(v_col[:, :], vT[:, ds(h, 1), :], ACT.Copy).then_inc(hd_vc, 1)
                    else:
                        act.wait_ge(hd_z, h + 1)
                        reach(act, hd_l, h)
                        A(zr[:, :], ps[:, 1, 0:3 * P], ACT.Relu).then_inc(hd_r, 1)
                        reach(act, hd_att, h)
                        A(wgt[:, :], ps[:, 1, 0:3 * P], ACT.Abs).then_inc(hd_r, 1)
                        act.wait_ge(hd_r, 5 * h + 2)
                        A(wgt[:, :], wgt[:, :], ACT.Exp, scale=-1.0).then_inc(hd_r, 1)
                        act.wait_ge(hd_r, 5 * h + 3)
                        A(wgt[:, :], wgt[:, :], ACT.Ln, bias=1.0).then_inc(hd_r, 1)

                def mid(i, j, q, k, p):
                    h = i + h0
                    if j == 0 and k == 1:
                        reach(act, hd_ssq, h + 1)
                        reach(act, hd_qn, 2 * h)
                        A(t2[:, :, :], ps[:, 0, :].rearrange("p (a t) -> p a t", a=2), ACT.Ln, scale=1.0 / HD,
                          bias=eps[:, 0:1]).then_inc(hd_ln, 1)
                        act.wait_ge(hd_ln, h + 1)
                        A(t2[:, :, :], t2[:, :, :], ACT.Exp, scale=-0.5).then_inc(hd_rs, 1)
                    if j == 0 and k == 2:
                        reach(act, hd_vt, h + 1)
                        reach(act, hd_att, h)
                        A(v_row[:, :, :], ps[:, 2, 0:S].rearrange("p (a d) -> p a d", a=TOK), ACT.Copy).then_inc(hd_vr, 1)
                    if j == 1 and k == 2:
                        reach(act, hd_tail, h + 1)
                        reach(act, hd_l, h + 1)
                        A(zr[:, :], ps[:, 1, 0:3 * P], ACT.Relu, scale=-1.0).then_inc(hd_r, 1)
                        act.wait_ge(hd_r, 5 * h + 5)
                        A(wgt[:, :], zr[:, :], ACT.Exp, scale=-1.0).then_inc(hd_e, 1)

                def post(i, j, q):
                    h = i + h0
                    if j == 1:
                        reach(act, hd_att, h + 1)
                        passed(act, act_passed)
                        A(att[:, ds(h, 1), 0, :], ps[:, 3:4, 0:S], ACT.Copy).then_inc(hd_ah, 1)
                return pre, mid, post

            act.preload_act_table_set("natural_log_exp_and_others")
            pre, mid, post = head(0)
            for part, name, first in ((HALF1, "GA1", 0), (HALF2, "GA2", NPW)):
                stage(P_GA, part, ada=ada_of(name, first), pre=pre, mid=mid, post=post, bias=T_GA)
            pre, mid, post = head(NT // 2)
            for part, name, first in ((HALF1, "GB1", 0), (HALF2, "GB2", NPW)):
                stage(P_GB, part, ada=ada_of(name, first), pre=pre, mid=mid, post=post, bias=T_GB)

            def gate_sig(i, j, q):
                for g in (1, 0):
                    act.wait_ge(evac_done, P_BR)
                    A(gates[:, g, ds(2 * q, 2), :], gates[:, g, ds(2 * q, 2), :], ACT.Sigmoid).then_inc(sga, 1)

            def b_half(i, j, q, k, p):
                if k == 1:
                    act.wait_ge(evac_done, p)
                    act.wait_ge(mm_done, CH * p + 2)
                    A(half[:, :, :], pm[:, 0:2, S:2 * S], ACT.Copy).then_inc(bhalf_done, 1)
                if k == 0 and not (isinstance(q, int) and q == 0):
                    merged_hi(q - 1)
                if k == 2:
                    reach(act, bevac_done, q + 1)
                    act.wait_ge(mm_done, CH * p + 4)
                    A(half[:, :, :], pm[:, 2:4, S:2 * S], ACT.Copy).then_inc(half_done, 1)

            def merged_hi(q):
                act.wait_ge(mrg, 2 * q + 2)
                passed(act, act_passed)
                A(actv[:, ds(2 * q, 2), 0, :], t2[:, :, :], ACT.Copy).then_inc(mrg_h, 1)
            act.preload_act_table(ACT.Sigmoid)
            for part, name, first in (([0, 1], "BR1", 0), (HALF2, "BR2", NPW)):
                stage(P_BR, part, ada=ada_of(name, first), pre=gate_sig, mid=b_half, evac=False)
            merged_hi(NPD - 1)

            def square(q):
                act.wait_ge(res, 3 * q + 3)
                reach(act, ssq2, q + 1)
                passed(act, act_passed)
                A(qn[:, :, :], xT[:, ds(2 * q, 2), :], ACT.Square).then_inc(sq2, 1)
            act.preload_act_table(ACT.Sqrt)
            def last_square(i, j, q, k, p):
                if k == 0 and not (isinstance(q, int) and q == 0):
                    square(q - 1)
            for part, name, first in (([0, 1], "OUT1", 0), (HALF2, "OUT2", NPW)):
                stage(P_OUT, part, ada=ada_of(name, first), mid=last_square)
            square(NPD - 1)
            reach(act, ssq2, NPD + 1)
            rms(ps[:, 0, 0:S])
            for n in range(KT):
                norm_hi(1, n)

            def hid_hi(n0):
                def f(i, j, q):
                    act.wait_ge(res, n0 + 2 * q + 2)
                    passed(act, act_passed)
                    A(hid[:, ds(2 * q, 2), 0, :], t2[:, :, :], ACT.Copy).then_inc(hid_h, 1)
                return f

            R0 = 3 * NPD
            RG = 4 * NPD
            for part, name, first in ((HALF1, "MI1", 0), (HALF2, "MI2", NPW)):
                stage(P_MLP, part, ada=ada_of(name, first), post=hid_hi(R0))
            stage(P_MLP + NPD, HALF1, ada=ada_of("MO1"))
            stage(P_MLP + NPD, HALF2, ada=ada_of("MO2", NPW))
            with act.Fori(1, GROUPS - 1) as g:
                stage(P_MLP + 2 * NPD * g, (0, BD), post=hid_hi(R0 + RG * g))
                stage(P_MLP + 2 * NPD * g + NPD, (0, BD))
            stage(P_MLP + 2 * NPD * (GROUPS - 1), (0, BD), post=hid_hi(R0 + RG * (GROUPS - 1)))

            PF = N_PANELS - NPD

            def out_copy(q, j):
                act.wait_ge(out_t, q + 1)
                reach(act, out_d[j], 16 * (q // 2) if isinstance(q, int) else 8 * (q - j))
                A(out_rows[:, j, :, :], ps[:, 1, :].rearrange("p (b n) -> p b n", b=TOK), ACT.Copy).then_inc(out_c, 1)

            for q in range(NPD):
                for k in range(CH):
                    if k == CH - 1:
                        if q > 0:
                            out_copy(q - 1, (q - 1) % 2)
                        half_copy((PF + q, q % 2))
                    if q + 1 < NPD:
                        hi_chunk(PF + q + 1, k)
            out_copy(NPD - 1, (NPD - 1) % 2)

        @block.vector
        def _(dve):
            V = nc.vector
            start(dve, [lru_m, hd_l, hd_qn, hd_al, bevac_done, mod_done, ssq2])
            n_small = [0]

            def chain(ins):
                n_small[0] += 1
                ins.then_inc(small, 1)
                dve.wait_ge(small, n_small[0])

            V.memset(ones[:, :], 1.0).then_inc(fills, 1)
            V.memset(vec_rows[:, :, :], 0.0).then_inc(vec_zero, 1)
            V.memset(eps[:, :], EPS).then_inc(fills, 1)
            V.memset(neg_one[:, :], -1.0).then_inc(fills, 1)

            for acc in ada_accs:
                chain(V.memset(acc[:, :], 0.0))
            dve.wait_ge(silu, 1)
            e = tiny[:, 0:2, :].rearrange("p a b -> p (a b)")
            chain(V.tensor_scalar(e, e, 1.0, None, ALU.add))
            chain(V.reciprocal(e, e))
            chain(V.tensor_tensor(c_act[:, :], ps[:, 3, 0:KT], e, ALU.mult))
            assert n_small[0] == SMALL_CACT
            def mod_add(n, bank, src_off, cc):
                dve.wait_ge(ada_sum, n + 1)
                dve.wait_ge(vec_c, 1)
                V.tensor_tensor(mod[:, ds(cc, AB // P)], ps[:, bank, src_off:src_off + AB // P],
                                cols[:, ds(C_BADA + cc, AB // P)], ALU.add).then_inc(mod_done, 1)

            def pro_block(n, after=None):
                acc = pro_acc[:, n % 2, :]
                for at, q in enumerate(DVE_Q):
                    dve.wait_ge(pro_in[q % 8], 16 * (2 * n + q // 8 + 1))
                    if q == 0:
                        V.tensor_scalar(acc, pro_w[:, 0, :], c_act[:, 0:1], None, ALU.mult).then_inc(ada_done, 1)
                    else:
                        dve.wait_ge(ada_done, n * len(DVE_Q) + at)
                        V.scalar_tensor_tensor(out=acc, in0=pro_w[:, q % 8, :], scalar=c_act[:, q:q + 1], in1=acc,
                                               op0=ALU.mult, op1=ALU.add).then_inc(ada_done, 1)
                    if at == 2 and n > 0:
                        mod_add(n - 1, 2, 0, PRO_ORDER[n - 1] * (AB // P))
                    if after:
                        after(at)

            def norm_scale(which):
                dve.wait_ge(rstd, 2 * which + 1)
                V.reciprocal(t3[:, 1, :], t3[:, 0, :]).then_inc(rstd, 1)
                dve.wait_ge(rstd, 2 * which + 2)

            def norm(which, tiles, steps=None):
                r0 = 2 * KT * which

                def buf(n):
                    return (t1, t2)[n % 4 // 2][:, n % 2, :]

                def scaled(n):
                    reach(dve, act_ready, r0 + n - 3 if n > 3 else 0)
                    V.scalar_tensor_tensor(out=buf(n), in0=xT[:, n, :], scalar=sg[:, which, n:n + 1],
                                           in1=t3[:, 1, :], op0=ALU.mult, op1=ALU.mult).then_inc(nrm_t, 1)

                def split(n):
                    sh = 3 * KT * which + n
                    dve.wait_ge(nrm_h, KT * which + n + 1)
                    V.scalar_tensor_tensor(out=actv[:, n, 1, :], in0=buf(n), scalar=mod[:, sh:sh + 1],
                                           in1=actv[:, n, 0, :].bitcast(F32), op0=ALU.add,
                                           op1=ALU.subtract).then_inc(act_ready, 1)

                for step in steps or range(len(tiles) + 2):
                    if step < len(tiles):
                        scaled(tiles[step])
                    if step >= 2:
                        split(tiles[step - 2])

            def lo_chunk(p, k):
                dve.wait_ge(hi_done, CH * p + k + 1)
                V.tensor_tensor(w_lo[:, k, :], raw[:, k, :], w_hi[:, k, :].bitcast(F32),
                                ALU.subtract).then_inc(lo_done, 1)

            def norm1_sg(i):
                dve.wait_ge(mod_done, 2 * i + 3)
                h0, h1 = i * (KT // 2), (i + 1) * (KT // 2)
                V.scalar_tensor_tensor(out=sg[:, 0, h0:h1], in0=mod[:, KT + h0:KT + h1], scalar=1.0,
                                       in1=cols[:, C_N1 + h0:C_N1 + h1], op0=ALU.add, op1=ALU.mult).then_inc(sg_done, 1)
                dve.wait_ge(sg_done, i + 1)

            pro_block(0)
            dve.wait_ge(silu, 3)
            lam = cols[:, C_LAM:C_LAM + NT]
            e, s, s2, acc = tiny[:, 3, :], tiny[:, 4, :], tiny[:, 5, :], tiny[:, 6, :]
            chain(V.tensor_scalar(s2, e, 2.0, None, ALU.add))
            chain(V.reciprocal(s2, s2))
            chain(V.tensor_tensor(s, e, s2, ALU.mult))
            chain(V.tensor_tensor(s2, s, s, ALU.mult))
            chain(V.tensor_scalar(acc, s2, 1.0 / (2 * N_SER - 1), 1.0 / (2 * N_SER - 3), ALU.mult, ALU.add))
            for n in range(N_SER - 3, -1, -1):
                chain(V.tensor_tensor(acc, acc, s2, ALU.mult))
                chain(V.tensor_scalar(acc, acc, 1.0 / (2 * n + 1), None, ALU.add))
            chain(V.tensor_tensor(acc, acc, s, ALU.mult))
            chain(V.tensor_scalar(s, lam, -1.0, 0.0, ALU.mult, ALU.max))
            chain(V.scalar_tensor_tensor(out=acc, in0=acc, scalar=2.0, in1=s, op0=ALU.mult, op1=ALU.add))
            chain(V.tensor_scalar(c8[:, :], acc, -LRU_C, None, ALU.mult))
            assert n_small[0] == SMALL_C8
            chain(V.tensor_scalar(gqk[:, 0:1], cols[:, C_GQ:C_GQ + 1], float(HD) ** -0.5, None, ALU.mult))
            chain(V.tensor_copy(gqk[:, 1:2], cols[:, C_GQ + 1:C_GQ + 2]))
            pro_block(1)

            def first_half(at):
                if at == 2:
                    norm1_sg(0)
                    norm_scale(0)
                if 3 <= at:
                    norm(0, range(KT // 2), steps=(at - 3,))
            pro_block(2, after=first_half)
            lo_chunk(0, 0)
            lo_chunk(0, 1)
            pro_block(3)
            lo_chunk(0, 2)
            mod_add(3, 2, 0, PRO_ORDER[3] * (AB // P))
            norm1_sg(1)
            norm(0, range(KT // 2, KT - KC))
            lo_chunk(0, 3)
            norm(0, range(KT - KC, KT))

            def ada_add(acc, a, m, kt0):
                dve.wait_ge(ada_in[a], 8 * (m + 2))
                dve.wait_ge(ada_done, PRO_ADA + m + a)
                V.scalar_tensor_tensor(out=acc[:, :], in0=ada_w[:, a, :],
                                       scalar=c_act[:, ds(kt0 + a, 1)], in1=acc[:, :],
                                       op0=ALU.mult, op1=ALU.add).then_inc(ada_done, 1)

            def ada_flush(n):
                mod_add(n, 2, 256, ADA_ORDER[n] * (AB // P))
                if n + 2 in ADA_ORDER:
                    chain(V.memset(ada_accs[n % 2][:, :], 0.0))

            def psum_sum(dst, b0, s):
                return V.tensor_tensor(dst, pm[:, b0:b0 + 2, 0:S], half[:, :, :], ALU.add).then_inc(s, 1)

            def stage(p0, bodies, ada=None, pre=None, mid=None, post=None, dst=None, used=None,
                      first=False):
                def body(i):
                    for j in range(2):
                        q = 2 * i + j
                        p = p0 + q
                        if pre:
                            pre(i, j, q, p)
                        for k in range(CH):
                            if k == CH - 1:
                                if dst is not None:
                                    if used:
                                        dve.wait_ge(res, used(q))
                                    dve.wait_ge(half_done, p + 1)
                                    psum_sum(dst(q), 2 * j, evac_done)
                                if post and first:
                                    post(i, j, q, p)
                            lo_chunk(p + 1, k)
                            if ada and k in (1, 2):
                                ada_add(ada_accs[ada[1] % 2], k - 1, ada[0] + 2 * q, ada[2] + 2 * q)
                            if mid:
                                mid(i, j, q, k, p)
                        if post and not first:
                            post(i, j, q, p)
                if isinstance(bodies, list):
                    for i in bodies:
                        body(i)
                else:
                    with dve.Fori(*bodies) as i:
                        body(i)

            HALF1, HALF2 = (0, BD // 2), (BD // 2, BD)
            stage(P_LX, [0, 1], ada=ada_of("LX"), dst=lambda q: lx[:, 2 * q:2 * q + 2, :])

            def conv(i, j, q, p):
                for n in range(2):
                    dve.wait_ge(conv_0, 2 * q + n + 1)
                    for d in range(1, TAPS):
                        if d > 1:
                            dve.wait_ge(conv_s, 6 * q + 3 * n + d - 1)
                        V.scalar_tensor_tensor(
                            out=lru_u[:, ds(2 * q + n, 1), d:S], in0=lx[:, ds(2 * q + n, 1), 0:S - d],
                            scalar=cols[:, ds(C_CW + (TAPS - 1 - d) * NT + 2 * q + n, 1)],
                            in1=lru_u[:, ds(2 * q + n, 1), d:S], op0=ALU.mult, op1=ALU.add).then_inc(conv_s, 1)
            stage(P_LG, (0, BW), ada=ada_of("LG"), pre=conv, dst=lambda q: lg[:, ds(2 * q, 2), :])

            def gate_u(i, j, q, p):
                reach(dve, ri_sig, 4 * q + 4)
                V.tensor_tensor(lru_iu[:, ds(2 * q, 2), :], lru_iu[:, ds(2 * q, 2), :],
                                lru_u[:, ds(2 * q, 2), :], ALU.mult)
            stage(P_Q, (0, BW), ada=ada_of("Q"), post=gate_u, dst=lambda q: qk[:, ds(2 * q, 2), 0, :])
            ada_flush(4)

            def mult2(i, j, q, p):
                tb = (t1, t2)[j]
                dve.wait_ge(lru_t, 5 * q + 5)
                V.reciprocal(tb[:, :, :], tb[:, :, :]).then_inc(lru_m, 1)
                reach(dve, lru_m, 2 * q + 1)
                V.scalar_tensor_tensor(out=lru_r[:, ds(2 * q, 2), :], in0=lru_r[:, ds(2 * q, 2), :], scalar=-2.0,
                                       in1=tb[:, :, :], op0=ALU.mult, op1=ALU.mult).then_inc(lru_m, 1)
            stage(P_K, (0, BW), post=mult2, dst=lambda q: qk[:, ds(2 * q, 2), 1, :])

            def scan(i, j, q, p):
                dve.wait_ge(lru_q, q + 1)
                V.tensor_tensor(lru_r[:, ds(2 * q, 2), :], lru_r[:, ds(2 * q, 2), :],
                                lru_iu[:, ds(2 * q, 2), :], ALU.mult).then_inc(lru_s, 1)
                dve.wait_ge(lru_s, 4 * q + 1)
                for n in range(2):
                    V.tensor_tensor_scan(flat(lru_u, (2 * q + n) * S, S), flat(lru_a, (2 * q + n) * S, S),
                                         flat(lru_r, (2 * q + n) * S, S), 0.0, ALU.mult,
                                         ALU.add).then_inc(lru_s, 1)
                dve.wait_ge(lru_s, 4 * q + 3)
                dve.wait_ge(gelu_done, 1)
                V.tensor_tensor(t1[:, :, :], lru_u[:, ds(2 * q, 2), :], lg[:, ds(2 * q, 2), :],
                                ALU.mult).then_inc(lru_s, 1)

            def rec_lo(i, j, q, p):
                dve.wait_ge(yb_hi, q + 1)
                V.tensor_tensor(yb[:, ds(2 * q, 2), 1, :], t1[:, :, :], yb[:, ds(2 * q, 2), 0, :].bitcast(F32),
                                ALU.subtract).then_inc(yb_ready, 1)
            stage(P_V, (0, BW), ada=ada_of("V"), pre=scan, post=rec_lo, dst=lambda q: vT[:, ds(2 * q, 2), :])

            def head(h0):
                def pre(i, j, q, p):
                    h = i + h0
                    if j == 1:
                        dve.wait_ge(hd_r, 5 * h + 4)
                        reach(dve, hd_tail, h)
                        V.tensor_tensor(lsum[:, :], zr[:, :], wgt[:, :], ALU.add).then_inc(hd_l, 1)

                def mid(i, j, q, k, p):
                    h = i + h0
                    if j == 0 and k == 1:
                        dve.wait_ge(hd_rs, h + 1)
                        for t in range(2):
                            V.scalar_tensor_tensor(out=qn[:, t:t + 1, :], in0=qk[:, ds(h, 1), t, :],
                                                   scalar=gqk[:, t:t + 1], in1=t2[:, t:t + 1, :],
                                                   op0=ALU.mult, op1=ALU.mult).then_inc(hd_qn, 1)

                def post(i, j, q, p):
                    h = i + h0
                    if j == 1:
                        dve.wait_ge(hd_ah, h + 1)
                        V.tensor_tensor(att[:, ds(h, 1), 1, :], ps[:, 3:4, 0:S],
                                        att[:, ds(h, 1), 0, :].bitcast(F32), ALU.subtract).then_inc(hd_al, 1)
                return pre, mid, post

            pre, mid, post = head(0)
            to_ga, to_gb = (lambda q: gates[:, 0, ds(2 * q, 2), :]), (lambda q: gates[:, 1, ds(2 * q, 2), :])
            stage(P_GA, HALF1, ada=ada_of("GA1"), pre=pre, mid=mid, post=post, dst=to_ga)
            ada_flush(5)
            stage(P_GA, HALF2, ada=ada_of("GA2", NPW), pre=pre, mid=mid, post=post, dst=to_ga)
            pre, mid, post = head(NT // 2)
            stage(P_GB, HALF1, ada=ada_of("GB1"), pre=pre, mid=mid, post=post, dst=to_gb)
            ada_flush(6)
            stage(P_GB, HALF2, ada=ada_of("GB2", NPW), pre=pre, mid=mid, post=post, dst=to_gb)

            def b_evac(i, j, q, k, p):
                if k == 1 and not (isinstance(q, int) and q == 0):
                    merged_lo(q - 1)
                if k == 1:
                    dve.wait_ge(bhalf_done, q + 1)
                    psum_sum(t1[:, :, :], 0, bevac_done)

            def merge(i, j, q, p):
                dve.wait_ge(half_done, p + 1)
                psum_sum(t2[:, :, :], 2, evac_done)
                dve.wait_ge(evac_done, p + 1)
                dve.wait_ge(sga, 2 * q + 2)
                V.tensor_tensor(t2[:, :, :], t2[:, :, :], gates[:, 0, ds(2 * q, 2), :], ALU.mult).then_inc(mrg, 1)
                dve.wait_ge(mrg, 2 * q + 1)
                dve.wait_ge(mrg_b, q + 1)
                V.tensor_tensor(t2[:, :, :], t2[:, :, :], t1[:, :, :], ALU.add).then_inc(mrg, 1)

            def merged_lo(q):
                dve.wait_ge(mrg_h, q + 1)
                V.tensor_tensor(actv[:, ds(2 * q, 2), 1, :], t2[:, :, :], actv[:, ds(2 * q, 2), 0, :].bitcast(F32),
                                ALU.subtract).then_inc(act_ready, 2)
            dve.wait_ge(hd_z, NT)
            reach(dve, hd_ssq, NT)
            V.memset(qn[:, :, :], 0.0).then_inc(zeros, 1)
            V.memset(t3[:, :, :], 0.0).then_inc(zeros, 1)
            stage(P_BR, [0, 1], ada=ada_of("BR1"), mid=b_evac, post=merge, first=True)
            ada_flush(7)
            stage(P_BR, HALF2, ada=ada_of("BR2", NPW), mid=b_evac, post=merge, first=True)
            merged_lo(NPD - 1)

            dve.wait_ge(act_ready, 2 * KT)

            dve.wait_ge(zeros, 2)

            def squares(i, j, q, k, p):
                if k == 1:
                    reach(dve, sq2, q)
                    reach(dve, ssq2, q)
                    V.tensor_tensor(t3[:, :, :], t3[:, :, :], qn[:, :, :], ALU.add).then_inc(ssq2, 1)

            def resid(i, j, q, p):
                dve.wait_ge(evac_done, p + 1)
                for n in range(2):
                    m = V.scalar_tensor_tensor(out=xT[:, ds(2 * q + n, 1), :], in0=t1[:, n:n + 1, :],
                                               scalar=mod[:, ds(2 * KT + 2 * q + n, 1)],
                                               in1=xT[:, ds(2 * q + n, 1), :], op0=ALU.mult, op1=ALU.add)
                    m.then_inc(res, 1 + n)
            stage(P_OUT, HALF1, ada=ada_of("OUT1"), mid=squares, post=resid, first=True, dst=lambda q: t1[:, :, :])
            ada_flush(8)
            dve.wait_ge(mod_done, 9)
            V.scalar_tensor_tensor(out=sg[:, 1, :], in0=mod[:, 4 * KT:5 * KT], scalar=1.0,
                                   in1=cols[:, C_N2:C_N2 + KT], op0=ALU.add, op1=ALU.mult).then_inc(sg_done, 1)
            dve.wait_ge(sg_done, 3)
            stage(P_OUT, HALF2, ada=ada_of("OUT2", NPW), mid=squares, post=resid, first=True, dst=lambda q: t1[:, :, :])
            dve.wait_ge(res, 3 * NPD)
            norm_scale(1)
            norm(1, range(KT // 2))
            mod_add(9, 2, 256, ADA_ORDER[9] * (AB // P))
            norm(1, range(KT // 2, KT))
            chain(V.memset(ada_accs[1][:, :], 0.0))
            dve.wait_ge(acc_zero, 1)

            R0 = 3 * NPD
            RG = 4 * NPD

            def relu2(n0, e0):
                def f(i, j, q, p):
                    dve.wait_ge(evac_done, p + 1)
                    V.scalar_tensor_tensor(out=t2[:, :, :], in0=t1[:, :, :], scalar=0.0, in1=t1[:, :, :],
                                           op0=ALU.max, op1=ALU.mult).then_inc(res, 2)
                    dve.wait_ge(hid_h, e0 + q + 1)
                    V.tensor_tensor(hid[:, ds(2 * q, 2), 1, :], t2[:, :, :],
                                    hid[:, ds(2 * q, 2), 0, :].bitcast(F32), ALU.subtract).then_inc(act_ready, 2)
                return f

            def accum(i, j, q, p):
                dve.wait_ge(evac_done, p + 1)
                V.tensor_tensor(mlp_acc[:, ds(2 * q, 2), :], mlp_acc[:, ds(2 * q, 2), :], t1[:, :, :],
                                ALU.add).then_inc(res, 2)

            to_t1 = lambda q: t1[:, :, :]
            def steps(g, half):
                return lambda q: R0 + RG * g + 2 * NPD * half + 2 * q
            stage(P_MLP, HALF1, ada=ada_of("MI1"), post=relu2(R0, 0), first=True, dst=to_t1, used=steps(0, 0))
            stage(P_MLP, HALF2, ada=ada_of("MI2", NPW), post=relu2(R0, 0), first=True, dst=to_t1, used=steps(0, 0))
            stage(P_MLP + NPD, HALF1, ada=ada_of("MO1"), post=accum, first=True, dst=to_t1, used=steps(0, 1))
            ada_flush(10)
            stage(P_MLP + NPD, HALF2, ada=ada_of("MO2", NPW), post=accum, first=True, dst=to_t1, used=steps(0, 1))
            with dve.Fori(1, GROUPS - 1) as g:
                stage(P_MLP + 2 * NPD * g, (0, BD), post=relu2(R0 + RG * g, NPD * g), first=True, dst=to_t1,
                      used=steps(g, 0))
                stage(P_MLP + 2 * NPD * g + NPD, (0, BD), post=accum, first=True, dst=to_t1, used=steps(g, 1))
            ada_flush(11)
            stage(P_MLP + 2 * NPD * (GROUPS - 1), (0, BD), post=relu2(R0 + RG * (GROUPS - 1), NPD * (GROUPS - 1)),
                  first=True, dst=to_t1, used=steps(GROUPS - 1, 0))

            PF = N_PANELS - NPD
            RF = R0 + RG * GROUPS - 2 * NPD
            for q in range(NPD):
                p = PF + q
                if q + 1 < NPD:
                    for k in range(CH):
                        lo_chunk(p + 1, k)
                dve.wait_ge(half_done, p + 1)
                dve.wait_ge(res, RF + 2 * q)
                psum_sum(t1[:, :, :], 2 * (q % 2), evac_done)
                dve.wait_ge(evac_done, p + 1)
                V.tensor_tensor(t1[:, :, :], t1[:, :, :], mlp_acc[:, 2 * q:2 * q + 2, :], ALU.add).then_inc(res, 1)
                dve.wait_ge(res, RF + 2 * q + 1)
                if q > 0:
                    dve.wait_ge(out_t, q)
                for n in range(2):
                    m = V.scalar_tensor_tensor(out=t2[:, n, :], in0=t1[:, n, :],
                                               scalar=mod[:, 5 * KT + 2 * q + n:5 * KT + 2 * q + n + 1],
                                               in1=xT[:, 2 * q + n, :], op0=ALU.mult, op1=ALU.add)
                m.then_inc(res, 1)

        @block.tensor
        def _(pe):
            MM = nc.tensor.matmul
            start(pe, [ri_mm, hd_ssq, hd_vt, hd_att, hd_tail])

            pe.wait_ge(consts, 2)
            pe.wait_ge(c_in, 16)
            MM(ps[:, 3, 0:KT], c_rows[0:KT, :], ident[0:KT, 0:KT], start=True, stop=True).then_inc(c_t, 1)
            def ada_sums(src, col, off, first, last, done):
                for t in range(AB // P):
                    m = MM(ps[:, 2, off + t:off + t + 1], src[:, t * P:(t + 1) * P], col,
                           start=(first == "each" or first and t == 0), stop=last, skip_group_check=True)
                m.then_inc(done, 1)

            def ada_reduce(n):
                pe.wait_ge(ada_done, PRO_ADA + (n + 1 - PRO_BLOCKS) * KT)
                reach(pe, mod_done, n)
                ada_sums(ada_accs[n % 2], ones[:, 0:1], 256, "each", True, ada_sum)

            def pro_chunk(n, q):
                if q == PE_Q[0]:
                    reach(pe, mod_done, n)
                    pe.wait_ge(small, SMALL_CACT)
                pe.wait_ge(pro_in[q % 8], 16 * (2 * n + q // 8 + 1))
                ada_sums(pro_w[:, q % 8, :], c_act[:, q:q + 1], 0, q == PE_Q[0], False, pro_mm)

            def pro_reduce(n):
                pe.wait_ge(ada_done, (n + 1) * len(DVE_Q))
                ada_sums(pro_acc[:, n % 2, :], ones[:, 0:1], 0, False, True, ada_sum)

            pro_chunk(0, PE_Q[0])
            pe.wait_ge(fills, 3)
            pe.wait_ge(vec_in, 16 * 11)
            for g in range(3):
                nc.tensor.transpose(ps[:, 0, g * P:(g + 1) * P], vec_rows[:, g, :], ident[:, :]).then_inc(vec_t, 1)
            def sum_x(b):
                pe.wait_ge(x_sq, b + 1)
                for t in range(2):
                    m = MM(ps[:, 1, 0:S], ones[:, :], (t1, t2)[b % 2][:, t, :], start=(b == 0 and t == 0),
                           stop=(b == KT // 2 - 1 and t == 1))
                m.then_inc(ssq, 1)

            for q in PE_Q[1:]:
                pro_chunk(0, q)
            pro_reduce(0)
            for b in range(TOK):
                pe.wait_ge(x_in[b], 16)
            for b in range(KT // 2):
                if b >= 4:
                    pe.wait_ge(x_c, b - 3)
                for t in range(2):
                    for k in range(TOK):
                        m = nc.tensor.transpose(pm[:, b % 4, t * S + k * P:t * S + (k + 1) * P],
                                                x_rows[:, k, (2 * b + t) * P:(2 * b + t + 1) * P], ident[:, :])
                m.then_inc(x_t, 1)
                if b >= 1:
                    sum_x(b - 1)
                if b == 3:
                    pro_chunk(1, PE_Q[0])
            sum_x(KT // 2 - 1)

            for q in PE_Q[1:]:
                pro_chunk(1, q)
            pro_reduce(1)

            def split_mm(bank, k, o, a, first, last):
                for hi in ((True, False) if first or not last else (False, True)):
                    if hi:
                        m = MM(pm[:, bank, :], w_hi[:, k, o:o + P], a, start=first, stop=last)
                    else:
                        m = MM(pm[:, bank, S:2 * S], w_lo[:, k, o:o + P], a[:, 0:S], start=False, stop=False,
                               skip_group_check=True)
                return m

            def panel(p, j, mov, ready=None, after=None, chunks=range(CH)):
                for k in chunks:
                    if ready:
                        ready(k, 0)
                    if k == 0:
                        reach(pe, evac_done, p - 1)
                    pe.wait_ge(lo_done, CH * p + k + 1)
                    for kk in range(KC):
                        if ready and kk:
                            ready(k, kk)
                        a = mov(KC * k + kk)
                        for t in range(2):
                            m = split_mm(2 * j + t, k, kk * PAN + t * P, a, k == 0 and kk == 0,
                                         k == CH - 1 and kk == KC - 1)
                    m.then_inc(mm_done, 1)
                    if after:
                        after(k)

            def mov_of(t):
                return lambda k: t[:, k, :, :].rearrange("p a t -> p (a t)")

            def stage(p0, bodies, mov, ready=None, after=None):
                def body(i):
                    for j in range(2):
                        q = 2 * i + j
                        panel(p0 + q, j, mov, ready, (lambda k: after(i, j, q, k)) if after else None)
                if isinstance(bodies, list):
                    for i in bodies:
                        body(i)
                else:
                    with pe.Fori(*bodies) as i:
                        body(i)

            def tiles_ready(base):
                return lambda k, kk: pe.wait_ge(act_ready, base + k * KC + kk + 1)

            h_mov = mov_of(actv)
            for n in (2, 3):
                for q in PE_Q:
                    pro_chunk(n, q)
                pro_reduce(n)
                if n == 2:
                    panel(P_LX, 0, h_mov, ready=tiles_ready(0), chunks=(0, 1))
            panel(P_LX, 0, h_mov, ready=tiles_ready(0), chunks=(2, 3))
            panel(P_LX + 1, 1, h_mov)
            stage(P_LX, [1], h_mov)
            stage(P_LG, (0, BW), h_mov)

            def ri(i, j, q, k):
                if k != 1:
                    return
                pe.wait_ge(lru_w_in, 32 * (q + 1))
                reach(pe, ri_sig, 4 * q)
                pe.wait_ge(conv_s, 6 * NPW)
                for n in range(2):
                    for g in range(2):
                        m = MM(ps[:, g, n * S:(n + 1) * S], lru_w[:, 2 * g + n, :], flat(lru_u, (2 * q + n) * S, S),
                               start=True, stop=True)
                m.then_inc(ri_mm, 1)
            stage(P_Q, (0, BW), h_mov, after=ri)
            ada_reduce(4)
            stage(P_K, (0, BW), h_mov)
            stage(P_V, (0, BW), h_mov)
            HALF1, HALF2 = (0, BD // 2), (BD // 2, BD)

            def head(h0, blocks):
                def f(i, j, q, k):
                    h = i + h0
                    if j == 0 and k == 0:
                        reach(pe, mod_done, blocks)
                        pe.wait_ge(hd_sq, h + 1)
                        MM(ps[:, 0, :], ones[:, :], t3[:, :, :].rearrange("p a t -> p (a t)"),
                           start=True, stop=True).then_inc(hd_ssq, 1)
                        pe.wait_ge(hd_vc, h + 1)
                        for b in range(TOK):
                            m = nc.tensor.transpose(ps[:, 2, b * P:(b + 1) * P], v_col[:, b * P:(b + 1) * P],
                                                    ident[:, :])
                        m.then_inc(hd_vt, 1)
                    if j == 0 and k == 3:
                        reach(pe, hd_qn, 2 * h + 2)
                        reach(pe, hd_e, h)
                        MM(ps[:, 1, 0:S], qn[:, 1, 0:P], qn[:, 0, :], start=True, stop=True)
                        MM(ps[:, 1, S:S + P], qn[:, 1, P:S], qn[:, 0, P:S], start=False, stop=True,
                           skip_group_check=True).then_inc(hd_z, 1)
                    if j == 1 and k == 1:
                        pe.wait_ge(hd_lm, h + 1)
                        MM(ps[:, 1, 0:S], neg_tri[:, :], lsum[:, 0:S], start=False, stop=True, skip_group_check=True)
                        MM(ps[:, 1, P:S], neg_one[:, :], lsum[:, S:S + P], start=False, stop=True,
                           skip_group_check=True)
                        MM(ps[:, 1, S:S + P], neg_tri[:, :], lsum[:, S:S + P], start=False, stop=True,
                           skip_group_check=True).then_inc(hd_tail, 1)
                    if j == 1 and k == 3:
                        pe.wait_ge(hd_w, h + 1)
                        pe.wait_ge(hd_vr, h + 1)
                        reach(pe, hd_al, h)
                        MM(ps[:, 3, 0:S], v_row[:, 0, :], wgt[:, 0:S], start=True, stop=True)
                        MM(ps[:, 3, P:S], v_row[:, 1, :], wgt[:, S:S + P], start=False, stop=True,
                           skip_group_check=True).then_inc(hd_att, 1)
                return f

            stage(P_GA, HALF1, h_mov, after=head(0, 5))
            ada_reduce(5)
            stage(P_GA, HALF2, h_mov, after=head(0, 6))
            stage(P_GB, HALF1, h_mov, after=head(NT // 2, 6))
            ada_reduce(6)
            stage(P_GB, HALF2, h_mov, after=head(NT // 2, 7))

            def branches(i):
                for j in range(2):
                    q = 2 * i + j
                    p = P_BR + q
                    for k in range(CH):
                        if k == 0:
                            pe.wait_ge(yb_ready, NPW)
                            pe.wait_ge(evac_done, P_BR - 1)
                            reach(pe, bevac_done, q)
                        if k == 2:
                            reach(pe, hd_al, NT)
                            pe.wait_ge(evac_done, p)
                        pe.wait_ge(lo_done, CH * p + k + 1)
                        mv = mov_of(yb if k < 2 else att)
                        b0 = 0 if k < 2 else 2
                        for kk in range(KC):
                            a = mv(KC * (k % 2) + kk)
                            for t in range(2):
                                m = split_mm(b0 + t, k, kk * PAN + t * P, a, k % 2 == 0 and kk == 0,
                                             k % 2 == 1 and kk == KC - 1)
                        m.then_inc(mm_done, 1)
            with pe.Fori(*HALF1) as i:
                branches(i)
            ada_reduce(7)
            with pe.Fori(*HALF2) as i:
                branches(i)

            rdy = tiles_ready(KT)

            def out_ready(k, kk):
                rdy(k, kk)
                if k == 0 and kk == 0:
                    reach(pe, bevac_done, NPD)
            stage(P_OUT, HALF1, h_mov, ready=out_ready)
            ada_reduce(8)
            stage(P_OUT, HALF2, h_mov)
            reach(pe, ssq2, NPD)
            for t in range(2):
                MM(ps[:, 0, 0:S], ones[:, :], t3[:, t, :], start=t == 0, stop=False)
            reach(pe, sq2, NPD)
            for t in range(2):
                m = MM(ps[:, 0, 0:S], ones[:, :], qn[:, t, :], start=False, stop=t == 1)
            m.then_inc(ssq2, 1)
            ada_reduce(9)

            AR = 2 * KT
            stage(P_MLP, HALF1, h_mov, ready=tiles_ready(AR))
            stage(P_MLP, HALF2, h_mov)
            hid_mov = mov_of(hid)
            stage(P_MLP + NPD, HALF1, hid_mov, ready=tiles_ready(AR + KT))
            ada_reduce(10)
            stage(P_MLP + NPD, HALF2, hid_mov)
            with pe.Fori(1, GROUPS - 1) as g:
                stage(P_MLP + 2 * NPD * g, (0, BD), h_mov)
                base = AR + KT + KT * g
                stage(P_MLP + 2 * NPD * g + NPD, (0, BD), hid_mov,
                      ready=tiles_ready(base))
            ada_reduce(11)
            g = GROUPS - 1
            stage(P_MLP + 2 * NPD * g, (0, BD), h_mov)
            base = AR + KT + KT * g
            PF = N_PANELS - NPD
            RF = 3 * NPD + 4 * NPD * GROUPS - 2 * NPD

            def out_rows_of(q):
                pe.wait_ge(res, RF + 2 * q + 2)
                reach(pe, out_c, q)
                for b in range(TOK):
                    for t in range(2):
                        m = nc.tensor.transpose(ps[:, 1, b * PAN + t * P:b * PAN + (t + 1) * P],
                                                t2[:, t, b * P:(b + 1) * P], ident[:, :])
                m.then_inc(out_t, 1)

            for q in range(NPD):
                panel(PF + q, q % 2, hid_mov, ready=tiles_ready(base),
                      after=lambda k: out_rows_of(q - 1) if k == 1 and q > 0 else None)
            out_rows_of(NPD - 1)


_INS = ['x', 'c', 'w_ada', 'b_ada', 'norm1_g', 'w_in', 'b_in', 'q_norm_g', 'k_norm_g', 'conv_w', 'conv_b',
        'w_rg', 'b_rg', 'w_ig', 'b_ig', 'lru_lambda', 'w_branch_a', 'w_branch_b', 'w_out', 'norm2_g',
        'w_mlp_in', 'w_mlp_out']


def kernel(**inputs):
    import numpy as _np
    import concourse.bacc as _bacc
    from concourse import mybir as _mybir
    from concourse.bass_utils import run_bass_kernel_spmd as _run

    nc = _bacc.Bacc("TRN2", target_bir_lowering=False, num_devices=1)
    arrays, args = {}, []
    for name in _INS:
        a = _np.ascontiguousarray(inputs[name])
        arrays[f"in_{name}_dram"] = a
        args.append(nc.dram_tensor(f"in_{name}_dram", a.shape, _mybir.dt.from_np(a.dtype), kind="ExternalInput").ap())
    shape = inputs["x"].shape
    args.append(nc.dram_tensor("out_dram", shape, _mybir.dt.float32, kind="ExternalOutput").ap())
    hybrid_block(nc, *args)
    r = _run(nc, [arrays], core_ids=[0])
    return r.results[0]["out_dram"]
```
